# Optimizing a Trainium2 kernel written in Bass

```python
import jax, jax.numpy as jnp
from jax import lax
import numpy as np

D_MODEL = 1024
BATCH = 1
SEQ = 256
DEPTH = 2

HGRN_HEADS = 4
HGRN_EXPAND = 128
HGRN_HEAD_V = 128
HGRN_KDIM = HGRN_HEADS * HGRN_EXPAND
HGRN_VDIM = HGRN_HEADS * HGRN_HEAD_V
HGRN_CHUNK = 64
MIN_FORGET = 1e-20

MOBA_HEADS = 8
MOBA_HEAD_DIM = 64
MOBA_DIM = MOBA_HEADS * MOBA_HEAD_DIM
MOBA_BLOCK = 256
MOBA_TOPK = 3
MOBA_Q_CHUNK = 32
MASK_VALUE = -1e9

D_FF = 2816
N_BRANCH = 2
NORM_EPS = 1e-6

IN_SIZES = (HGRN_KDIM, HGRN_KDIM, HGRN_VDIM, HGRN_VDIM, MOBA_DIM, MOBA_DIM, MOBA_DIM, N_BRANCH * D_MODEL)
D_IN = int(sum(IN_SIZES))
IN_SPLITS = tuple(int(v) for v in np.cumsum(IN_SIZES)[:-1])

kernel_name = 'hybrid_hgrn2_moba_macaron'

def rmsnorm(x, w):
    xf = x.astype(jnp.float32)
    y = xf * lax.rsqrt(jnp.mean(xf * xf, axis=-1, keepdims=True) + NORM_EPS)
    return (y * w.astype(jnp.float32)).astype(x.dtype)

def swiglu(h, w_gu, w_down):
    gate, up = jnp.split(h @ w_gu, 2, axis=-1)
    return (jax.nn.silu(gate) * up) @ w_down

def alibi_slopes(n_heads):
    return jnp.exp2(-8.0 * jnp.arange(1, n_heads + 1, dtype=jnp.float32) / n_heads)

def hgrn2_mix(q, f_logit, i, g, lower_bound, norm_w):
    B, S, _ = q.shape
    H, dk, dv, C = HGRN_HEADS, HGRN_EXPAND, HGRN_HEAD_V, HGRN_CHUNK
    NC = S // C
    qf = jax.nn.silu(q.astype(jnp.float32))
    fl = f_logit.astype(jnp.float32)
    lb = jnp.clip(lower_bound.astype(jnp.float32), 0.0, 1.0)
    sig = jax.nn.sigmoid(fl)
    f = lb + (1.0 - lb) * sig
    log_f = jnp.log(jnp.maximum(f, MIN_FORGET))
    kf = (1.0 - lb) * (1.0 - sig)
    inp = i.astype(jnp.float32)

    def to_chunks(t, hd):
        return t.reshape(B, NC, C, H, hd).transpose(1, 0, 3, 2, 4)

    causal = jnp.tril(jnp.ones((C, C), dtype=bool))

    def step(state, xs):
        qc, kc, lfc, ic = xs
        b = jnp.cumsum(lfc, axis=2)
        rel = b[:, :, :, None, :] - b[:, :, None, :, :]
        decay = jnp.where(causal[:, :, None], jnp.exp(jnp.minimum(rel, 0.0)), 0.0)
        attn = jnp.einsum('bhtd,bhtsd,bhsd->bhts', qc, decay, kc)
        o = (jnp.einsum('bhts,bhsv->bhtv', attn, ic)
             + jnp.einsum('bhtd,bhdv->bhtv', qc * jnp.exp(b), state))
        b_last = b[:, :, -1:, :]
        state = (jnp.exp(b_last[:, :, 0, :])[..., None] * state
                 + jnp.einsum('bhsd,bhsv->bhdv', kc * jnp.exp(b_last - b), ic))
        return state, o

    state0 = jnp.zeros((B, H, dk, dv), jnp.float32)
    xs = (to_chunks(qf, dk), to_chunks(kf, dk), to_chunks(log_f, dk), to_chunks(inp, dv))
    _, o = lax.scan(step, state0, xs)
    o = o.transpose(1, 0, 3, 2, 4).reshape(B, S, H, dv)
    o = o * lax.rsqrt(jnp.mean(o * o, axis=-1, keepdims=True) + NORM_EPS) * norm_w.astype(jnp.float32)
    o = o * jax.nn.silu(g.astype(jnp.float32).reshape(B, S, H, dv))
    return o.reshape(B, S, HGRN_VDIM).astype(q.dtype)

def moba_mix(q, k, v):
    B, S, _ = q.shape
    H, Dh, BS, QC = MOBA_HEADS, MOBA_HEAD_DIM, MOBA_BLOCK, MOBA_Q_CHUNK
    S_pad = -(-S // BS) * BS
    NB = S_pad // BS
    kt = min(MOBA_TOPK, NB)
    nqc = S_pad // QC
    scale = Dh ** -0.5
    pad = ((0, 0), (0, S_pad - S), (0, 0))

    def heads(t):
        return jnp.pad(t, pad).reshape(B, S_pad, H, Dh).transpose(0, 2, 1, 3)

    qh, kh, vh = heads(q), heads(k), heads(v)
    k_blocks = kh.reshape(B, H, NB, BS, Dh)
    v_blocks = vh.reshape(B, H, NB, BS, Dh)

    k_mean = jnp.mean(k_blocks.astype(jnp.float32), axis=3)
    gate = jnp.einsum('bhsd,bhnd->bhsn', qh.astype(jnp.float32), k_mean)
    q_block = jnp.arange(S_pad) // BS
    past = jnp.arange(NB)[None, :] < q_block[:, None]
    gate = jnp.where(past, gate, MASK_VALUE)
    _, sel = lax.top_k(gate, kt)
    sel_valid = jnp.arange(kt)[None, :] < jnp.minimum(q_block, kt)[:, None]

    q_ch = qh.reshape(B, H, nqc, QC, Dh).transpose(2, 0, 1, 3, 4)
    sel_ch = sel.reshape(B, H, nqc, QC, kt).transpose(2, 0, 1, 3, 4)
    valid_ch = sel_valid.reshape(nqc, QC, kt)
    gather_blocks = jax.vmap(jax.vmap(lambda blk, ix: blk[ix]))
    slopes = alibi_slopes(H)

    def attend(args):
        c, qc, ic, vc = args
        t_pos = c * QC + jnp.arange(QC)
        own_start = (c * QC // BS) * BS
        k_own = lax.dynamic_slice_in_dim(kh, own_start, BS, axis=2)
        v_own = lax.dynamic_slice_in_dim(vh, own_start, BS, axis=2)
        k_sel = gather_blocks(k_blocks, ic)
        v_sel = gather_blocks(v_blocks, ic)
        dist_sel = (t_pos[None, None, :, None, None]
                    - (ic[..., None] * BS + jnp.arange(BS))).astype(jnp.float32)
        s_sel = (jnp.einsum('bhtd,bhtrkd->bhtrk', qc, k_sel, preferred_element_type=jnp.float32) * scale
                 - slopes[None, :, None, None, None] * jnp.abs(dist_sel))
        s_sel = jnp.where(vc[:, :, None], s_sel, MASK_VALUE)
        dist_own = t_pos[:, None] - (own_start + jnp.arange(BS))[None, :]
        s_own = (jnp.einsum('bhtd,bhkd->bhtk', qc, k_own, preferred_element_type=jnp.float32) * scale
                 - slopes[None, :, None, None] * jnp.abs(dist_own).astype(jnp.float32))
        s_own = jnp.where(dist_own >= 0, s_own, MASK_VALUE)
        scores = jnp.concatenate([s_sel.reshape(B, H, QC, kt * BS), s_own], axis=-1)
        p = jax.nn.softmax(scores, axis=-1)
        p_sel = p[..., :kt * BS].reshape(B, H, QC, kt, BS)
        p_own = p[..., kt * BS:]
        out = (jnp.einsum('bhtrk,bhtrkd->bhtd', p_sel, v_sel.astype(jnp.float32))
               + jnp.einsum('bhtk,bhkd->bhtd', p_own, v_own.astype(jnp.float32)))
        return out.astype(q.dtype)

    out = lax.map(attend, (jnp.arange(nqc, dtype=jnp.int32), q_ch, sel_ch, valid_ch))
    out = out.transpose(1, 2, 0, 3, 4).reshape(B, H, S_pad, Dh)[:, :, :S]
    return out.transpose(0, 2, 1, 3).reshape(B, S, MOBA_DIM)

def setup_inputs(seed: int = 0) -> dict:
    key = jax.random.key(seed)
    ks = jax.random.split(key, 16)
    f32 = jnp.float32

    def w(k, shape, fan_in):
        return jax.random.normal(k, shape, f32) * (fan_in ** -0.5)

    def gain(k, shape):
        return 1.0 + 0.01 * jax.random.normal(k, shape, f32)

    return {
        'x': jax.random.normal(ks[0], (BATCH, SEQ, D_MODEL), f32),
        'ffn1_norm': gain(ks[1], (DEPTH, D_MODEL)),
        'ffn1_w_gu': w(ks[2], (DEPTH, D_MODEL, 2 * D_FF), D_MODEL),
        'ffn1_w_down': w(ks[3], (DEPTH, D_FF, D_MODEL), D_FF),
        'mix_norm': gain(ks[4], (DEPTH, D_MODEL)),
        'w_in': w(ks[5], (DEPTH, D_MODEL, D_IN), D_MODEL),
        'hgrn_lb_logits': 0.5 * jax.random.normal(ks[6], (DEPTH, HGRN_KDIM), f32),
        'hgrn_norm': gain(ks[7], (DEPTH, HGRN_HEAD_V)),
        'w_branch_a': w(ks[8], (DEPTH, HGRN_VDIM, D_MODEL), HGRN_VDIM),
        'w_branch_b': w(ks[9], (DEPTH, MOBA_DIM, D_MODEL), MOBA_DIM),
        'w_out': w(ks[10], (DEPTH, D_MODEL, D_MODEL), D_MODEL),
        'ffn2_norm': gain(ks[11], (DEPTH, D_MODEL)),
        'ffn2_w_gu': w(ks[12], (DEPTH, D_MODEL, 2 * D_FF), D_MODEL),
        'ffn2_w_down': w(ks[13], (DEPTH, D_FF, D_MODEL), D_FF),
        'final_norm': gain(ks[14], (D_MODEL,)),
    }

def reference(x, ffn1_norm, ffn1_w_gu, ffn1_w_down, mix_norm, w_in, hgrn_lb_logits, hgrn_norm,
              w_branch_a, w_branch_b, w_out, ffn2_norm, ffn2_w_gu, ffn2_w_down, final_norm):
    lb_sm = jax.nn.softmax(hgrn_lb_logits.astype(jnp.float32), axis=0)
    lower_bounds = jnp.cumsum(lb_sm, axis=0) - lb_sm[0]
    for l in range(DEPTH):
        x = x + 0.5 * swiglu(rmsnorm(x, ffn1_norm[l]), ffn1_w_gu[l], ffn1_w_down[l])
        h = rmsnorm(x, mix_norm[l])
        hq, hf, hi, hg, mq, mk, mv, gates = jnp.split(h @ w_in[l], IN_SPLITS, axis=-1)
        o_a = hgrn2_mix(hq, hf, hi, hg, lower_bounds[l], hgrn_norm[l])
        o_b = moba_mix(mq, mk, mv)
        gate_a, gate_b = jnp.split(jax.nn.sigmoid(gates), 2, axis=-1)
        merged = gate_a * (o_a @ w_branch_a[l]) + gate_b * (o_b @ w_branch_b[l])
        x = x + merged @ w_out[l]
        x = x + 0.5 * swiglu(rmsnorm(x, ffn2_norm[l]), ffn2_w_gu[l], ffn2_w_down[l])
    return rmsnorm(x, final_norm)


_drawn_inputs = setup_inputs


def setup_inputs(seed=0):
    import zlib

    import numpy as np

    out = dict(_drawn_inputs(seed))
    spreads = {}
    factors = {'ffn1_norm': 8.0,
     'mix_norm': 7.631,
     'hgrn_lb_logits': 3.721,
     'hgrn_norm': 8.0,
     'ffn2_norm': 8.0,
     'final_norm': 5.757}
    for name, (base, spread) in spreads.items():
        noise = np.random.default_rng([zlib.crc32(name.encode()), seed]).standard_normal(out[name].shape)
        drawn = base * np.exp(spread * noise) if base else spread * noise
        out[name] = __import__('jax').numpy.asarray(drawn.astype(out[name].dtype))
    for name, factor in factors.items():
        out[name] = (out[name] * factor).astype(out[name].dtype)
    return out
```

```python
from contextlib import ExitStack

import concourse.bass as bass
from concourse import mybir

F32 = mybir.dt.float32
F32R = mybir.dt.float32r
I32 = mybir.dt.int32
ALU = mybir.AluOpType
ACT = mybir.ActivationFunctionType
AX = mybir.AxisListType.X

P = 128
DEPTH = 2
D = 1024
KT = D // P
S = 256
TT = S // P
FF = 2816
UC = 256
US = KT * UC
FJ = FF // UC
HH = 4
MH = 8
MD = 64
SW = 3 * P
EPS = 1e-6
MIN_FORGET = 1e-20
LEVELS = 9
NMASK = 8

HQ, HF, HI, HG, MQ, MK, MV, GATE = 0, 512, 1024, 1536, 2048, 2560, 3072, 3584
IN_COLS = [c + UC * i for c in (HF, HQ, MQ, MK, MV, HI, HG) for i in range(2)] + [GATE + UC * i for i in range(8)]
U_HF, U_HQ, U_MQ, U_MK, U_MV, U_HI, U_HG, U_GATE = 0, 2, 4, 6, 8, 10, 12, 14
NIN = len(IN_COLS)
U_A, U_B, U_WO = NIN, NIN + 2, NIN + 4
NMIX = NIN + 8
PER_LAYER = 2 * FJ + NMIX // 3
BASE = (0, FJ, FJ + NMIX // 3)
NORMS = 3

PR = 3 * KT + 1 + HH
C_NORM, C_HN, C_LB, C_OML, C_NOML = (0, KT, 2 * KT), 3 * KT, 3 * KT + 1, 3 * KT + 5, 3 * KT + 9
PC = 3 * KT + 13


def build(nc, x, ffn1_norm, ffn1_w_gu, ffn1_w_down, mix_norm, w_in, lb_logits, hgrn_norm, w_a, w_b, w_out,
          ffn2_norm, ffn2_w_gu, ffn2_w_down, final_norm, shape_consts, out):
    with ExitStack() as ctx:
        def sb(name, shape, dt=F32):
            return ctx.enter_context(nc.sbuf_tensor(name, shape, dt))

        def sem(name):
            return ctx.enter_context(nc.semaphore(name))

        raw = [sb(f"raw{s}", [P, US]) for s in range(3)]
        high = [sb(f"high{s}", [P, US], F32R) for s in range(3)]
        low = [sb(f"low{s}", [P, US], F32R) for s in range(3)]
        xs = sb("xs", [P, TT, D])
        xn = sb("xn", [P, TT, D])
        act_h = sb("act_h", [P, KT, S], F32R)
        act_l = sb("act_l", [P, KT, S], F32R)
        br_h = sb("br_h", [P, KT, S], F32R)
        br_l = sb("br_l", [P, KT, S], F32R)
        gates = sb("gates", [P, 2 * KT, S])
        q_sb = sb("q_sb", [P, HH * S])
        k_sb = sb("k_sb", [P, HH * S])
        f_sb = sb("f_sb", [P, HH * S])
        t_sb = sb("t_sb", [P, HH * S])
        at = sb("at", [P, 3, HH, P])
        hg_sb = sb("hg_sb", [P, TT, HH * P])
        mq_sb = sb("mq_sb", [P, HH, S])
        mk_sb = sb("mk_sb", [P, HH, S])
        s_sb = sb("s_sb", [P, 2, SW])
        pt_sb = sb("pt_sb", [P, 2, SW])
        alibi = sb("alibi", [P, MH, SW])
        consts = sb("consts", [P, P + SW + NMASK * P])
        fnorm = sb("fnorm", [P, D])
        rows = sb("rows", [DEPTH * PR, P])
        par = sb("par", [P, DEPTH, PC])
        cur = sb("cur", [P, PC])
        lbt = sb("lbt", [P, 6, HH])
        neg_half = sb("neg_half", [P, 2 * HH])
        ssq = sb("ssq", [P, TT])
        msq = sb("msq", [P, TT])
        rstd = sb("rstd", [P, TT])
        hsq = sb("hsq", [P, 2 * HH])
        hms = sb("hms", [P, 2 * HH])
        hrs = sb("hrs", [P, 2 * HH])
        nmax = sb("nmax", [P, 2, 2])
        psums = sb("psums", [P, 2, 2])
        prec = sb("prec", [P, 2, 2])

        bank = [ctx.enter_context(nc.psum_tensor(f"bank{i}", [P, 2, S], F32)) for i in range(8)]

        ident = consts[:, 0:P]
        distance = consts[:, P:P + SW]
        masks = consts[:, P + SW:].bitcast(I32).rearrange("p (m t) -> p m t", m=NMASK)
        inp = xn[:, 0, :].rearrange("p (t v) -> p t v", t=TT)
        val = xn[:, 1, :].rearrange("p (t v) -> p t v", t=TT)
        silu_g = gates[:, 0:2, :]
        prod = gates[:, 2:4, :]
        o_sb = t_sb[:].rearrange("p (t v) -> p t v", t=TT)
        T_BANKS = (0, 1, 6, 7)

        raw_loaded = [sem(f"raw_loaded{s}") for s in range(3)]
        high_ready = [sem(f"high_ready{s}") for s in range(3)]
        low_ready = [sem(f"low_ready{s}") for s in range(3)]
        unit_done = [sem(f"unit_done{s}") for s in range(3)]
        x_loaded = sem("x_loaded")
        consts_loaded = sem("consts_loaded")
        rows_loaded = sem("rows_loaded")
        neg_half_set = sem("neg_half_set")
        rows_turned = sem("rows_turned")
        par_copied = sem("par_copied")
        lb_step = sem("lb_step")
        lb_diff = sem("lb_diff")
        lb_exp = sem("lb_exp")
        par_ready = sem("par_ready")
        cur_ready = sem("cur_ready")
        alibi_ready = sem("alibi_ready")
        at_zeroed = sem("at_zeroed")
        x_new = sem("x_new")
        ssq_ready = sem("ssq_ready")
        msq_ready = sem("msq_ready")
        rstd_ready = sem("rstd_ready")
        xn_ready = sem("xn_ready")
        xn_turned = sem("xn_turned")
        act_high = sem("act_high")
        act_low = sem("act_low")
        silu_ready = sem("silu_ready")
        prod_ready = sem("prod_ready")
        prod_high = sem("prod_high")
        prod_low = sem("prod_low")
        half_done = sem("half_done")
        evicted = sem("evicted")
        forget_raw = sem("forget_raw")
        decays_ready = sem("decays_ready")
        level_done = sem("level_done")
        level_seen = sem("level_seen")
        level_taken = sem("level_taken")
        level_t = sem("level_t")
        level_next = sem("level_next")
        o_done = sem("o_done")
        o_squared = sem("o_squared")
        o_summed = sem("o_summed")
        o_ms = sem("o_ms")
        o_rstd = sem("o_rstd")
        o_scaled = sem("o_scaled")
        hg_ready = sem("hg_ready")
        gates_ready = sem("gates_ready")
        o_gated = sem("o_gated")
        o_turned = sem("o_turned")
        o_high = sem("o_high")
        o_low = sem("o_low")
        scores_done = sem("scores_done")
        s_biased = sem("s_biased")
        s_max = sem("s_max")
        s_exp = sem("s_exp")
        s_rec = sem("s_rec")
        p_ready = sem("p_ready")
        p_turned = sem("p_turned")
        pt_ready = sem("pt_ready")
        pv_done = sem("pv_done")
        ob_high = sem("ob_high")
        ob_low = sem("ob_low")
        gated_b = sem("gated_b")
        merged = sem("merged")
        merged_high = sem("merged_high")
        merged_low = sem("merged_low")
        y_ready = sem("y_ready")
        out_stored = sem("out_stored")

        gu_v = [w.rearrange("l (k p) n -> l p k n", p=P) for w in (ffn1_w_gu, ffn2_w_gu)]
        down_v = [w.rearrange("l (j k p) n -> l j p k n", p=P, k=2) for w in (ffn1_w_down, ffn2_w_down)]
        in_v = w_in.rearrange("l (k p) n -> l p k n", p=P)
        branch_v = [w.rearrange("l (k p) n -> l p k n", p=P) for w in (w_a, w_b)]
        wo_v = w_out.rearrange("l (j k p) n -> l j p k n", p=P, k=2)

        block = ctx.enter_context(nc.Block())

        @block.sync
        def _(sp):
            def load(s, n, dst, src):
                sp.wait_ge(low_ready[s], n + 1)
                sp.dma_start(dst, src).then_inc(raw_loaded[s], 16)

            def load_gu(f, l, j, s):
                src = gu_v[f][bass.ds(l, 1), :, :, bass.ds(j * UC + s * FF, UC)].rearrange("l p k n -> p (l k) n")
                load(s, l * PER_LAYER + BASE[2 * f] + j, raw[s][:].rearrange("p (k n) -> p k n", k=KT), src)

            def load_down(f, l, j):
                src = down_v[f][bass.ds(l, 1), bass.ds(j, 1)].rearrange("l j p k n -> p (l j k) n")
                load(2, l * PER_LAYER + BASE[2 * f] + j, raw[2][:].rearrange("p (k n) -> p k n", k=2), src)

            def load_mix(l, u):
                if u < NIN:
                    src = in_v[bass.ds(l, 1), :, :, IN_COLS[u]:IN_COLS[u] + UC].rearrange("l p k n -> p (l k) n")
                elif u < U_WO:
                    w, half = divmod(u - U_A, 2)
                    src = branch_v[w][bass.ds(l, 1), :, :, half * 512:half * 512 + 512].rearrange("l p k n -> p (l k) n")
                elif u < NMIX:
                    src = wo_v[bass.ds(l, 1), u - U_WO].rearrange("l p k n -> p (l k) n")
                else:
                    load_gu(1, l, 0, u - NMIX)
                    return
                load(u % 3, l * PER_LAYER + BASE[1] + u // 3,
                     raw[u % 3][:].rearrange("p (k n) -> p k n", k=src.shape[1]), src)

            def ffn(f, l):
                with sp.Fori(0, FJ - 1) as j:
                    load_gu(f, l, j + 1, 0)
                    load_gu(f, l, j + 1, 1)
                    load_down(f, l, j)
                if f == 0:
                    load_mix(l, 0)
                    load_mix(l, 1)
                load_down(f, l, FJ - 1)

            with sp.Fori(0, DEPTH) as l:
                load_gu(0, l, 0, 0)
                load_gu(0, l, 0, 1)
                ffn(0, l)
                for u in range(2, NMIX + 2):
                    load_mix(l, u)
                ffn(1, l)

        @block.gpsimd
        def _(pool):
            for s in range(3):
                pool.sem_inc(low_ready[s], 1)
                pool.sem_inc(unit_done[s], 1)
            pool.sem_inc(prod_low, 1)
            pool.dma_start(xn[:], x[0].rearrange("(t p) d -> p t d", p=P)).then_inc(x_loaded, 16)
            for l in range(DEPTH):
                at_row = l * PR
                for src, n in ((ffn1_norm, KT), (mix_norm, KT), (ffn2_norm, KT), (hgrn_norm, 1), (lb_logits, HH)):
                    pool.dma_start(rows[at_row:at_row + n, :],
                                   src[l].rearrange("(k p) -> k p", p=P)).then_inc(rows_loaded, 16)
                    at_row += n
            pool.dma_start(consts[:], shape_consts).then_inc(consts_loaded, 16)
            pool.dma_start(fnorm[:], final_norm.partition_broadcast(P)).then_inc(consts_loaded, 16)
            pool.memset(neg_half[:], -0.5).then_inc(neg_half_set, 1)
            pool.wait_ge(neg_half_set, 1)

            def norm(r):
                for t in range(TT):
                    pool.wait_ge(msq_ready, r * TT + (t + 1))
                    pool.tensor_tensor(rstd[:, t:t + 1], msq[:, t:t + 1], neg_half[:, t:t + 1],
                                       ALU.pow).then_inc(rstd_ready, 1)

            with pool.Fori(0, DEPTH) as l:
                norm(l * NORMS)
                norm(l * NORMS + 1)
                pool.wait_ge(o_ms, l + 1)
                pool.tensor_tensor(hrs[:], hms[:], neg_half[:], ALU.pow).then_inc(o_rstd, 1)
                norm(l * NORMS + 2)
            norm(DEPTH * NORMS)
            for t in range(TT):
                pool.wait_ge(y_ready, t + 1)
                pool.dma_start(out[0, t * P:(t + 1) * P, :], xn[:, t, :]).then_inc(out_stored, 16)
            pool.wait_ge(out_stored, 16 * TT)

        @block.scalar
        def _(act):
            def split(s, n):
                act.wait_ge(raw_loaded[s], n * 16 + 16)
                act.wait_ge(unit_done[s], n + 1)
                act.activation(high[s][:], raw[s][:], ACT.Copy).then_inc(high_ready[s], 1)

            def split_mix(l, u):
                split(u % 3, l * PER_LAYER + BASE[1] + u // 3)

            def square_sums(r):
                for t in range(TT):
                    act.wait_ge(x_new, r * TT + (t + 1))
                    act.activation(xn[:, t, :], xs[:, t, :], ACT.Square,
                                   accum_out=ssq[:, t:t + 1]).then_inc(ssq_ready, 1)

            def norm(l, i):
                r = l * NORMS + i
                square_sums(r)
                for b in range(4):
                    act.wait_ge(xn_turned, r * 4 + (b + 1))
                    for e in range(2):
                        kt = 2 * b + e
                        ins = act.activation(act_h[:, kt, :], bank[T_BANKS[b]][:, e, :], ACT.Copy,
                                             scale=cur[:, C_NORM[i] + kt:C_NORM[i] + kt + 1])
                    ins.then_inc(act_high, 1)

            def ffn(f, l):
                base = l * PER_LAYER + BASE[2 * f]
                q = (l * 2 + f) * FJ

                def silu(j):
                    act.wait_ge(unit_done[0], base + j + 2)
                    act.activation(silu_g, bank[0][:], ACT.Silu).then_inc(silu_ready, 1)

                def product_high(j):
                    act.wait_ge(prod_ready, q + j + 1)
                    act.wait_ge(unit_done[2], base + j + 1)
                    act.activation(br_h[:, 0:2, :], prod, ACT.Copy).then_inc(prod_high, 1)

                with act.Fori(0, FJ - 1) as j:
                    silu(j)
                    split(0, base + j + 1)
                    split(1, base + j + 1)
                    product_high(j)
                    split(2, base + j)
                silu(FJ - 1)
                if f == 0:
                    split_mix(l, 0)
                    split_mix(l, 1)
                product_high(FJ - 1)
                split(2, base + (FJ - 1))

            def mixer(l):
                def evict(u):
                    act.wait_ge(unit_done[u % 3], l * PER_LAYER + (BASE[1] + u // 3 + 2))
                    src = bank[u % 2][:]
                    func, e = ACT.Copy, u % 2
                    if u < U_HQ:
                        func, dst = ACT.Sigmoid, t_sb[:, 512 * e:512 * e + 512].rearrange("p (h t) -> p h t", h=2)
                    elif u < U_MQ:
                        func, dst = ACT.Silu, q_sb[:, 512 * e:512 * e + 512].rearrange("p (h t) -> p h t", h=2)
                    elif u < U_MK:
                        dst = mq_sb[:, 2 * e:2 * e + 2, :]
                    elif u < U_MV:
                        dst = mk_sb[:, 2 * e:2 * e + 2, :]
                    elif u < U_HI:
                        dst = val[:, :, UC * e:UC * e + UC]
                    elif u < U_HG:
                        dst = inp[:, :, UC * e:UC * e + UC]
                    elif u < U_GATE:
                        dst = hg_sb[:, :, UC * e:UC * e + UC]
                    else:
                        g = u - U_GATE
                        dst = gates[:, 2 * g:2 * g + 2, :]
                        func = ACT.Copy if g < 3 else ACT.Sigmoid
                    act.activation(dst, src, func).then_inc(evicted, 1)

                def softmax_exp(h):
                    b = h % 2
                    act.wait_ge(s_max, l * MH + (h + 1))
                    act.activation(s_sb[:, b, 0:P], s_sb[:, b, 0:P], ACT.Exp, bias=nmax[:, b, 0:1],
                                   accum_out=psums[:, b, 0:1])
                    act.activation(s_sb[:, b, P:SW], s_sb[:, b, P:SW], ACT.Exp, bias=nmax[:, b, 1:2],
                                   accum_out=psums[:, b, 1:2]).then_inc(s_exp, 1)

                def probs_copy(h):
                    act.wait_ge(p_turned, l * MH + (h + 1))
                    if h >= 2:
                        act.wait_ge(pv_done, l * MH + (h - 1))
                    act.activation(pt_sb[:, h % 2, :], bank[4 + h % 2][:].rearrange("p a b -> p (a b)")[:, 0:SW],
                                   ACT.Copy).then_inc(pt_ready, 1)

                for u in range(U_WO):
                    split_mix(l, u + 2)
                    if u == 14:
                        act.wait_ge(o_done, l + 1)
                        for t in range(TT):
                            ins = act.activation(o_sb[:, t, :], bank[2 + t][:].rearrange("p a b -> p (a b)"),
                                                 ACT.Square)
                        ins.then_inc(o_squared, 1)
                    if 10 <= u < 10 + MH:
                        probs_copy(u - 10)
                    if u < NIN:
                        evict(u)
                    if 8 <= u < 8 + MH:
                        softmax_exp(u - 8)
                    if u == 16:
                        act.wait_ge(evicted, l * NIN + U_GATE)
                        act.activation(hg_sb[:], hg_sb[:], ACT.Silu).then_inc(hg_ready, 1)
                        act.wait_ge(evicted, l * NIN + (U_GATE + 3))
                        act.activation(gates[:, 0:6, :], gates[:, 0:6, :], ACT.Sigmoid).then_inc(gates_ready, 1)
                    if u == 19:
                        for b in range(2):
                            act.wait_ge(pv_done, l * MH + 4 * (b + 1))
                            act.activation(br_h[:, 4 + 2 * b:6 + 2 * b, :], bank[6 + b][:],
                                           ACT.Copy).then_inc(ob_high, 1)
                    if u == 20:
                        act.wait_ge(o_turned, l + 1)
                        for b in range(2):
                            act.activation(br_h[:, 2 * b:2 * b + 2, :], bank[2 + b][:], ACT.Copy,
                                           scale=cur[:, C_HN:C_HN + 1]).then_inc(o_high, 1)
                for u in range(U_WO, NMIX):
                    split_mix(l, u + 2)
                    if u < U_WO + 2:
                        half = u - U_WO
                        act.wait_ge(merged, l * 2 + (half + 1))
                        act.activation(act_h[:, 4 * half:4 * half + 4, :], gates[:, 4 * half:4 * half + 4, :],
                                       ACT.Copy).then_inc(merged_high, 1)

            act.wait_ge(consts_loaded, 32)
            for h in range(MH):
                ins = act.activation(alibi[:, h, :], distance, ACT.Copy, scale=2.0 ** (-8.0 * (h + 1) / MH))
            ins.then_inc(alibi_ready, 1)
            act.wait_ge(lb_diff, 1)
            act.activation(lbt[:, 1:3, :], lbt[:, 1:3, :], ACT.Exp).then_inc(lb_exp, 1)
            with act.Fori(0, DEPTH) as l:
                split(0, l * PER_LAYER)
                split(1, l * PER_LAYER)
                act.wait_ge(cur_ready, l + 1)
                norm(l, 0)
                ffn(0, l)
                norm(l, 1)
                mixer(l)
                norm(l, 2)
                ffn(1, l)
            square_sums(DEPTH * NORMS)

        @block.vector
        def _(dve):
            def split(s, n):
                dve.wait_ge(high_ready[s], n + 1)
                dve.tensor_tensor(low[s][:], raw[s][:], high[s][:].bitcast(F32),
                                  ALU.subtract).then_inc(low_ready[s], 1)

            def split_mix(l, u):
                split(u % 3, l * PER_LAYER + BASE[1] + u // 3)

            def normalise(r):
                for t in range(TT):
                    dve.wait_ge(ssq_ready, r * TT + (t + 1))
                    dve.tensor_scalar(msq[:, t:t + 1], ssq[:, t:t + 1], 1.0 / D, EPS, ALU.mult,
                                      ALU.add).then_inc(msq_ready, 1)

            def norm(l, i):
                r = l * NORMS + i
                normalise(r)
                for t in range(TT):
                    dve.wait_ge(rstd_ready, r * TT + (t + 1))
                    dve.tensor_scalar(xn[:, t, :], xs[:, t, :], rstd[:, t:t + 1], None,
                                      ALU.mult).then_inc(xn_ready, 1)
                for b in range(4):
                    dve.wait_ge(act_high, r * 4 + (b + 1))
                    for e in range(2):
                        kt = 2 * b + e
                        ins = dve.scalar_tensor_tensor(act_l[:, kt, :], bank[T_BANKS[b]][:, e, :],
                                                       cur[:, C_NORM[i] + kt:C_NORM[i] + kt + 1],
                                                       act_h[:, kt, :].bitcast(F32), ALU.mult, ALU.subtract)
                    ins.then_inc(act_low, 1)

            def residual(l, i, scale, last_slot_value):
                for t in range(TT):
                    if t == 0:
                        dve.wait_ge(half_done, l * 3 + (i + 1))
                    else:
                        dve.wait_ge(unit_done[2], last_slot_value)
                    for n in range(2):
                        v = xs[:, t, 512 * n:512 * n + 512]
                        ins = dve.scalar_tensor_tensor(v, bank[2 + 2 * t + n][:].rearrange("p a b -> p (a b)"),
                                                       scale, v, ALU.mult, ALU.add)
                    ins.then_inc(x_new, 1)

            def ffn(f, l):
                base = l * PER_LAYER + BASE[2 * f]
                q = (l * 2 + f) * FJ

                def product(j):
                    dve.wait_ge(silu_ready, q + j + 1)
                    dve.wait_ge(unit_done[1], base + j + 2)
                    dve.wait_ge(prod_low, q + j + 1)
                    dve.tensor_tensor(prod, bank[1][:], silu_g, ALU.mult).then_inc(prod_ready, 1)

                def product_low(j):
                    dve.wait_ge(prod_high, q + j + 1)
                    dve.tensor_tensor(br_l[:, 0:2, :], prod, br_h[:, 0:2, :].bitcast(F32),
                                      ALU.subtract).then_inc(prod_low, 1)

                with dve.Fori(0, FJ - 1) as j:
                    split(0, base + j + 1)
                    product(j)
                    split(1, base + j + 1)
                    product_low(j)
                    split(2, base + j)
                if f == 0:
                    split_mix(l, 0)
                product(FJ - 1)
                if f == 0:
                    split_mix(l, 1)
                product_low(FJ - 1)
                split(2, base + (FJ - 1))
                residual(l, 2 * f, 0.5, base + (FJ + 1))

            def mixer(l):
                def level(i):
                    m = 1 if i == 0 else 1 << (i - 1)
                    dve.wait_ge(level_done, l * LEVELS + (i + 1))
                    dve.sem_inc(level_seen, 1)
                    if i == LEVELS - 1:
                        dve.tensor_copy(at[:, 2], bank[2][:].rearrange("p a (b t) -> p (a b) t", b=2)
                                        ).then_inc(level_taken, 1)
                        return
                    for t in range(TT):
                        ins = dve.copy_predicated(at[:, t], masks[:, i:i + 1, :].to_broadcast([P, HH, P]),
                                                  bank[2 + t][:].rearrange("p a (b t) -> p (a b) t", b=2))
                    if i == 0:
                        dve.tensor_tensor(q_sb[:], q_sb[:], f_sb[:], ALU.mult).then_inc(level_taken, 1)
                        return
                    n = HH * S // m
                    tm = f_sb[:] if m == 1 else t_sb[:, HH * S - 2 * n:HH * S - n]
                    tb = tm.rearrange("p (g e) -> p g e", e=2)
                    qv = q_sb[:].rearrange("p (g e m) -> p g e m", e=2, m=m)
                    kv = k_sb[:].rearrange("p (g e m) -> p g e m", e=2, m=m)
                    if m > 1:
                        dve.wait_ge(level_t, l * (LEVELS - 3) + (i - 1))
                    if i < LEVELS - 2:
                        dve.tensor_tensor(t_sb[:, HH * S - n:HH * S - n // 2], tb[:, :, 0], tb[:, :, 1],
                                          ALU.mult).then_inc(level_t, 1)
                    dve.tensor_tensor(kv[:, :, 0, :], kv[:, :, 0, :], tb[:, :, 1:2].to_broadcast([P, n // 2, m]), ALU.mult)
                    dve.tensor_tensor(qv[:, :, 1, :], qv[:, :, 1, :], tb[:, :, 0:1].to_broadcast([P, n // 2, m]),
                                      ALU.mult).then_inc(level_taken, 1)

                def scores_max(h):
                    b = h % 2
                    dve.wait_ge(scores_done, l * MH + (h + 1))
                    if h >= 2:
                        dve.wait_ge(p_turned, l * MH + (h - 1))
                    dve.scalar_tensor_tensor(s_sb[:, b, :], bank[4 + b][:].rearrange("p a b -> p (a b)")[:, 0:SW],
                                             float(MD) ** -0.5, alibi[:, h, :], ALU.mult, ALU.add).then_inc(s_biased, 1)
                    dve.wait_ge(s_biased, l * MH + (h + 1))
                    dve.tensor_reduce(nmax[:, b, 0:1], s_sb[:, b, 0:P], AX, ALU.max, negate=True)
                    dve.tensor_reduce(nmax[:, b, 1:2], s_sb[:, b, P:SW], AX, ALU.max, negate=True).then_inc(s_max, 1)

                def probs_scale(h):
                    b = h % 2
                    dve.wait_ge(s_exp, l * MH + (h + 1))
                    dve.reciprocal(prec[:, b, :], psums[:, b, :]).then_inc(s_rec, 1)
                    dve.wait_ge(s_rec, l * MH + (h + 1))
                    dve.tensor_scalar(s_sb[:, b, 0:P], s_sb[:, b, 0:P], prec[:, b, 0:1], None, ALU.mult)
                    dve.tensor_scalar(s_sb[:, b, P:SW], s_sb[:, b, P:SW], prec[:, b, 1:2], None,
                                      ALU.mult).then_inc(p_ready, 1)

                for u in range(NMIX):
                    split_mix(l, u + 2)
                    if u == 2:
                        dve.wait_ge(evicted, l * NIN + 2)
                        for h in range(HH):
                            v = slice(h * S, h * S + S)
                            oml = cur[:, C_OML + h:C_OML + h + 1]
                            ins = dve.tensor_scalar(f_sb[:, v], t_sb[:, v], oml, cur[:, C_LB + h:C_LB + h + 1],
                                                    ALU.mult, ALU.add)
                            dve.tensor_scalar(k_sb[:, v], t_sb[:, v], 1.0, cur[:, C_NOML + h:C_NOML + h + 1],
                                              ALU.subtract, ALU.mult)
                        ins.then_inc(forget_raw, 1)
                        dve.wait_ge(forget_raw, l + 1)
                        dve.tensor_scalar(f_sb[:], f_sb[:], MIN_FORGET, None, ALU.max).then_inc(decays_ready, 1)
                    if 8 <= u < 8 + MH:
                        scores_max(u - 8)
                    if 4 <= u < 4 + LEVELS:
                        if u == 4:
                            dve.wait_ge(decays_ready, l + 1)
                        level(u - 4)
                    if u == 15:
                        dve.wait_ge(o_squared, l + 1)
                        dve.tensor_reduce(hsq[:], t_sb[:].rearrange("p (g v) -> p g v", v=P), AX,
                                          ALU.add).then_inc(o_summed, 1)
                        dve.wait_ge(o_summed, l + 1)
                        dve.tensor_scalar(hms[:], hsq[:], 1.0 / P, EPS, ALU.mult, ALU.add).then_inc(o_ms, 1)
                    if u == 16:
                        dve.wait_ge(o_rstd, l + 1)
                        for t in range(TT):
                            ins = dve.tensor_tensor(o_sb[:, t, :].rearrange("p (h v) -> p h v", h=HH),
                                                    bank[2 + t][:].rearrange("p a (b v) -> p (a b) v", b=2),
                                                    hrs[:, HH * t:HH * t + HH].rearrange("p (h e) -> p h e", e=1)
                                                    .to_broadcast([P, HH, P]), ALU.mult)
                        ins.then_inc(o_scaled, 1)
                    if u == 17:
                        dve.wait_ge(o_scaled, l + 1)
                        dve.wait_ge(hg_ready, l + 1)
                        dve.tensor_tensor(o_sb[:], o_sb[:], hg_sb[:], ALU.mult).then_inc(o_gated, 1)
                    if 8 <= u < 8 + MH:
                        probs_scale(u - 8)
                    if u == 19:
                        for b in range(2):
                            dve.wait_ge(ob_high, l * 2 + (b + 1))
                            dve.tensor_tensor(br_l[:, 4 + 2 * b:6 + 2 * b, :], bank[6 + b][:],
                                              br_h[:, 4 + 2 * b:6 + 2 * b, :].bitcast(F32),
                                              ALU.subtract).then_inc(ob_low, 1)
                    if u == 20:
                        for b in range(2):
                            dve.wait_ge(o_high, l * 2 + (b + 1))
                            dve.scalar_tensor_tensor(br_l[:, 2 * b:2 * b + 2, :], bank[2 + b][:], cur[:, C_HN:C_HN + 1],
                                                     br_h[:, 2 * b:2 * b + 2, :].bitcast(F32), ALU.mult,
                                                     ALU.subtract).then_inc(o_low, 1)
                    if u in (U_A, U_A + 1):
                        half = u - U_A
                        dve.wait_ge(unit_done[u % 3], l * PER_LAYER + (BASE[1] + u // 3 + 2))
                        if half == 0:
                            dve.wait_ge(evicted, l * NIN + NIN)
                            dve.wait_ge(gates_ready, l + 1)
                        for b in range(2):
                            g = gates[:, 4 * half + 2 * b:4 * half + 2 * b + 2, :]
                            dve.tensor_tensor(g, g, bank[2 * half + b][:], ALU.mult)
                    if u in (U_B, U_B + 1):
                        half = u - U_B
                        dve.wait_ge(unit_done[u % 3], l * PER_LAYER + (BASE[1] + u // 3 + 2))
                        for b in range(2):
                            g = gates[:, KT + 4 * half + 2 * b:KT + 4 * half + 2 * b + 2, :]
                            ins = dve.tensor_tensor(g, g, bank[4 + 2 * half + b][:], ALU.mult)
                        ins.then_inc(gated_b, 1)
                        dve.wait_ge(gated_b, l * 2 + (half + 1))
                        ga = gates[:, 4 * half:4 * half + 4, :]
                        dve.tensor_tensor(ga, ga, gates[:, KT + 4 * half:KT + 4 * half + 4, :],
                                          ALU.add).then_inc(merged, 1)
                    if u in (U_WO, U_WO + 1):
                        half = u - U_WO
                        dve.wait_ge(merged_high, l * 2 + (half + 1))
                        dve.tensor_tensor(act_l[:, 4 * half:4 * half + 4, :], gates[:, 4 * half:4 * half + 4, :],
                                          act_h[:, 4 * half:4 * half + 4, :].bitcast(F32),
                                          ALU.subtract).then_inc(merged_low, 1)
                residual(l, 1, 1.0, l * PER_LAYER + (BASE[1] + (NMIX - 1) // 3 + 2))

            dve.memset(at[:], 0.0).then_inc(at_zeroed, 1)
            dve.wait_ge(x_loaded, 16)
            for t in range(TT):
                dve.tensor_copy(xs[:, t, :], xn[:, t, :]).then_inc(x_new, 1)
            dve.wait_ge(rows_turned, 1)
            pr = bank[7][:].rearrange("p a b -> p (a b)")[:, 0:DEPTH * PR].rearrange("p (l c) -> p l c", l=DEPTH)
            dve.tensor_copy(par[:, :, 0:PR], pr).then_inc(par_copied, 1)
            dve.wait_ge(par_copied, 1)
            lg = par[:, :, C_LB:C_LB + HH]
            dve.tensor_tensor(lbt[:, 0, :], lg[:, 0], lg[:, 1], ALU.max).then_inc(lb_step, 1)
            dve.wait_ge(lb_step, 1)
            for i in range(DEPTH):
                ins = dve.tensor_tensor(lbt[:, 1 + i, :], lg[:, i], lbt[:, 0, :], ALU.subtract)
            ins.then_inc(lb_diff, 1)
            dve.wait_ge(lb_exp, 1)
            dve.tensor_tensor(lbt[:, 3, :], lbt[:, 1, :], lbt[:, 2, :], ALU.add).then_inc(lb_step, 1)
            dve.wait_ge(lb_step, 2)
            dve.reciprocal(lbt[:, 0, :], lbt[:, 3, :]).then_inc(lb_step, 1)
            dve.wait_ge(lb_step, 3)
            for i in range(DEPTH):
                ins = dve.tensor_tensor(lbt[:, 4 + i, :], lbt[:, 1 + i, :], lbt[:, 0, :], ALU.mult)
            ins.then_inc(lb_step, 1)
            dve.wait_ge(lb_step, 4)
            dve.tensor_tensor(lbt[:, 3, :], lbt[:, 4, :], lbt[:, 5, :], ALU.add).then_inc(lb_step, 1)
            dve.wait_ge(lb_step, 5)
            dve.tensor_tensor(lg[:, 0], lbt[:, 4, :], lbt[:, 4, :], ALU.subtract)
            dve.tensor_tensor(lg[:, 1], lbt[:, 3, :], lbt[:, 4, :], ALU.subtract).then_inc(lb_step, 1)
            dve.wait_ge(lb_step, 6)
            dve.tensor_scalar(lg, lg, 0.0, 1.0, ALU.max, ALU.min).then_inc(lb_step, 1)
            dve.wait_ge(lb_step, 7)
            dve.tensor_scalar(par[:, :, C_OML:C_OML + HH], lg, -1.0, 1.0, ALU.mult, ALU.add)
            dve.tensor_scalar(par[:, :, C_NOML:C_NOML + HH], lg, 1.0, None, ALU.subtract).then_inc(par_ready, 1)
            dve.wait_ge(par_ready, 1)
            dve.wait_ge(at_zeroed, 1)
            dve.wait_ge(consts_loaded, 32)
            dve.wait_ge(alibi_ready, 1)
            with dve.Fori(0, DEPTH) as l:
                dve.tensor_copy(cur[:], par[:, bass.ds(l, 1), :].rearrange("p l c -> p (l c)")).then_inc(cur_ready, 1)
                split(0, l * PER_LAYER)
                dve.wait_ge(cur_ready, l + 1)
                norm(l, 0)
                split(1, l * PER_LAYER)
                ffn(0, l)
                norm(l, 1)
                mixer(l)
                norm(l, 2)
                ffn(1, l)
            normalise(DEPTH * NORMS)
            for t in range(TT):
                dve.wait_ge(rstd_ready, DEPTH * NORMS * TT + t + 1)
                dve.scalar_tensor_tensor(xn[:, t, :], xs[:, t, :], rstd[:, t:t + 1], fnorm[:], ALU.mult,
                                         ALU.mult).then_inc(y_ready, 1)

        @block.tensor
        def _(pe):
            def products(dst, left, right, first, last):
                pe.matmul(dst, left[0], right[0], start=first, stop=False)
                pe.matmul(dst, left[0], right[1], start=False, stop=False)
                return pe.matmul(dst, left[1], right[0], start=False, stop=last)

            def act_pair(k, cols):
                return act_h[:, k, cols], act_l[:, k, cols]

            def br_pair(k, cols):
                return br_h[:, k, cols], br_l[:, k, cols]

            def w_pair(s, start, n):
                return high[s][:, start:start + n], low[s][:, start:start + n]

            def cols(t):
                return slice(t * P, t * P + P)

            ALL = slice(0, S)

            def norm_turns(l, i):
                r = l * NORMS + i
                for b in range(4):
                    if b == 0:
                        pe.wait_ge(xn_ready, r * TT + TT)
                    for e in range(2):
                        for t in range(TT):
                            kt = 2 * b + e
                            ins = pe.transpose(bank[T_BANKS[b]][:, e, cols(t)], xn[:, t, kt * P:kt * P + P], ident)
                    ins.then_inc(xn_turned, 1)

            def wide_unit(s, n, dst, norm=None, token_major=False):
                pe.wait_ge(low_ready[s], n + 2)
                for g in range(2):
                    for k in range(KT):
                        if norm is not None and g == 0 and k % 2 == 0:
                            pe.wait_ge(act_low, norm * 4 + (k // 2 + 1))
                        if token_major:
                            ins = products(dst[:, g, :], act_pair(k, cols(g)), w_pair(s, k * UC, UC), k == 0, k == KT - 1)
                        else:
                            ins = products(dst[:, g, :], w_pair(s, k * UC + g * P, P), act_pair(k, ALL), k == 0,
                                           k == KT - 1)
                ins.then_inc(unit_done[s], 1)

            def residual_unit(s, n, pair, k0, first, last):
                pe.wait_ge(low_ready[s], n + 2)
                for t in range(TT):
                    for h in range(2):
                        for e in range(2):
                            ins = products(bank[2 + 2 * t + h][:].rearrange("p a b -> p (a b)"), pair(k0 + e, cols(t)),
                                           w_pair(s, e * D + h * 512, 512), first and e == 0, last and e == 1)
                    if last and t == 0:
                        ins.then_inc(half_done, 1)
                ins.then_inc(unit_done[s], 1)

            def ffn(f, l):
                base = l * PER_LAYER + BASE[2 * f]
                q = (l * 2 + f) * FJ

                def gate(j, norm=None):
                    if norm is None:
                        pe.wait_ge(silu_ready, q + j)
                    wide_unit(0, base + j, bank[0], norm)

                def up(j, first=False):
                    if not first:
                        pe.wait_ge(prod_ready, q + j)
                    wide_unit(1, base + j, bank[1])

                def down(j, first=False, last=False):
                    pe.wait_ge(prod_low, q + j + 2)
                    residual_unit(2, base + j, br_pair, 0, first, last)

                gate(0, l * NORMS + 2 * f)
                up(0, True)
                gate(1)
                up(1)
                down(0, first=True)
                with pe.Fori(2, FJ) as j:
                    gate(j)
                    up(j)
                    down(j - 1)
                down(FJ - 1, last=True)

            def mixer(l):
                def level(i):
                    if i == 0:
                        pe.wait_ge(evicted, l * NIN + U_MQ)
                        pe.wait_ge(decays_ready, l + 1)
                    else:
                        pe.wait_ge(level_taken, l * LEVELS + i)
                    if i == LEVELS - 1:
                        for h in range(HH):
                            ins = pe.matmul(bank[2][:, h // 2, cols(h % 2)], k_sb[:, h * S:h * S + P],
                                            q_sb[:, h * S + P:h * S + S], start=True, stop=True)
                    else:
                        for t in range(TT):
                            for h in range(HH):
                                v = slice(h * S + t * P, h * S + t * P + P)
                                ins = pe.matmul(bank[2 + t][:, h // 2, cols(h % 2)], k_sb[:, v], q_sb[:, v],
                                                start=True, stop=True)
                    ins.then_inc(level_done, 1)

                def hgrn_out():
                    pe.wait_ge(level_taken, l * LEVELS + LEVELS)
                    pe.wait_ge(evicted, l * NIN + U_HG)
                    for h in range(HH):
                        v = slice(h * P, h * P + P)
                        pe.matmul(bank[2][:, h // 2, cols(h % 2)], at[:, 0, h, :], inp[:, 0, v], start=True, stop=True)
                    for h in range(HH):
                        v = slice(h * P, h * P + P)
                        pe.matmul(bank[3][:, h // 2, cols(h % 2)], at[:, 2, h, :], inp[:, 0, v], start=True, stop=False)
                        ins = pe.matmul(bank[3][:, h // 2, cols(h % 2)], at[:, 1, h, :], inp[:, 1, v], start=False,
                                        stop=True)
                    ins.then_inc(o_done, 1)

                def hgrn_turns():
                    pe.wait_ge(o_gated, l + 1)
                    for h in range(HH):
                        for t in range(TT):
                            ins = pe.transpose(bank[2 + h // 2][:, h % 2, cols(t)], o_sb[:, t, h * P:h * P + P], ident)
                    ins.then_inc(o_turned, 1)

                def scores(h):
                    if h == 0:
                        pe.wait_ge(evicted, l * NIN + U_MV)
                    if h >= 2:
                        pe.wait_ge(pt_ready, l * MH + (h - 1))
                    v = slice(MD * (h % 2), MD * (h % 2) + MD)
                    b = bank[4 + h % 2][:].rearrange("p a b -> p (a b)")
                    pe.matmul(b[:, 0:P], mq_sb[v, h // 2, 0:P], mk_sb[v, h // 2, 0:P], start=True, stop=True)
                    pe.matmul(b[:, P:SW], mq_sb[v, h // 2, P:S], mk_sb[v, h // 2, :], start=True,
                              stop=True).then_inc(scores_done, 1)

                def probs_turns(h):
                    pe.wait_ge(p_ready, l * MH + (h + 1))
                    b = bank[4 + h % 2][:].rearrange("p a b -> p (a b)")
                    for c in range(3):
                        ins = pe.transpose(b[:, cols(c)], s_sb[:, h % 2, cols(c)], ident)
                    ins.then_inc(p_turned, 1)

                def values(h):
                    if h == 0:
                        pe.wait_ge(evicted, l * NIN + U_HI)
                    pe.wait_ge(pt_ready, l * MH + (h + 1))
                    dst = bank[6 + h // 4][MD * (h % 2):MD * (h % 2) + MD, (h // 2) % 2, :]
                    v = slice(MD * h, MD * h + MD)
                    pe.matmul(dst, val[:, 0, v], pt_sb[:, h % 2, 0:S], start=True, stop=False)
                    pe.matmul(dst[:, P:S], val[:, 1, v], pt_sb[:, h % 2, S:SW], start=False,
                              stop=True).then_inc(pv_done, 1)

                for u in range(NMIX):
                    s, n = u % 3, l * PER_LAYER + (BASE[1] + u // 3)
                    if u < NIN:
                        if u >= 2:
                            pe.wait_ge(evicted, l * NIN + (u - 1))
                        wide_unit(s, n, bank[u % 2], l * NORMS + 1 if u == 0 else None,
                                  U_MV <= u < U_GATE)
                    elif u < U_WO:
                        half = (u - U_A) % 2
                        if u == U_A:
                            pe.wait_ge(o_low, l * 2 + 2)
                            pe.wait_ge(evicted, l * NIN + NIN)
                        if u == U_B:
                            pe.wait_ge(ob_low, l * 2 + 2)
                        pe.wait_ge(low_ready[s], n + 2)
                        b0, k0 = (0, 0) if u < U_B else (4, 4)
                        for m in range(4):
                            for k in range(4):
                                ins = products(bank[b0 + 2 * half + m // 2][:, m % 2, :], w_pair(s, k * 512 + m * P, P),
                                               br_pair(k0 + k, ALL), k == 0, k == 3)
                        ins.then_inc(unit_done[s], 1)
                    else:
                        i = u - U_WO
                        if i % 2 == 0:
                            pe.wait_ge(merged_low, l * 2 + (i // 2 + 1))
                        residual_unit(s, n, act_pair, 2 * i, i == 0, i == 3)
                    if 10 <= u < 10 + MH:
                        values(u - 10)
                    if 9 <= u < 9 + MH:
                        probs_turns(u - 9)
                    if 8 <= u < 8 + MH:
                        scores(u - 8)
                    if 4 <= u < 4 + LEVELS:
                        level(u - 4)
                    if u == 13:
                        hgrn_out()
                    if u == 19:
                        hgrn_turns()

            pe.wait_ge(rows_loaded, 160)
            pe.wait_ge(consts_loaded, 32)
            pe.transpose(bank[7][:].rearrange("p a b -> p (a b)")[:, 0:DEPTH * PR], rows[:],
                         ident[0:DEPTH * PR, 0:DEPTH * PR]).then_inc(rows_turned, 1)
            with pe.Fori(0, DEPTH) as l:
                norm_turns(l, 0)
                ffn(0, l)
                norm_turns(l, 1)
                mixer(l)
                norm_turns(l, 2)
                ffn(1, l)


_INS = ['x', 'ffn1_norm', 'ffn1_w_gu', 'ffn1_w_down', 'mix_norm', 'w_in', 'hgrn_lb_logits', 'hgrn_norm', 'w_branch_a',
        'w_branch_b', 'w_out', 'ffn2_norm', 'ffn2_w_gu', 'ffn2_w_down', 'final_norm']


def kernel(**inputs):
    import numpy as _np
    import concourse.bacc as _bacc
    from concourse.bass_utils import run_bass_kernel_spmd as _run

    nc = _bacc.Bacc("TRN2", target_bir_lowering=False, num_devices=1)
    arrays, args = {}, []
    for name in _INS:
        a = _np.ascontiguousarray(inputs[name])
        arrays[f"in_{name}"] = a
        args.append(nc.dram_tensor(f"in_{name}", a.shape, mybir.dt.from_np(a.dtype), kind="ExternalInput").ap())
    key, query = _np.arange(P)[None, :], _np.arange(P)[:, None]
    same = key - query
    causal = _np.where(same <= 0, same, -4e11)
    src, dst = query, key
    masks = [src == dst]
    for i in range(NMASK - 1):
        m = 1 << i
        masks.append((src // (2 * m) == dst // (2 * m)) & (src // m % 2 == 0) & (dst // m % 2 == 1))
    consts = _np.concatenate([_np.eye(P), causal, same - P, causal] + masks, axis=1).astype(_np.float32)
    arrays["shape_consts"] = consts
    args.append(nc.dram_tensor("shape_consts", consts.shape, F32, kind="ExternalInput").ap())
    args.append(nc.dram_tensor("out_0", (1, S, D), F32, kind="ExternalOutput").ap())
    build(nc, *args)
    r = _run(nc, [arrays], core_ids=[0])
    return r.results[0]["out_0"]
```

```python
from contextlib import ExitStack

import concourse.bass as bass
from concourse import mybir

F32 = mybir.dt.float32
F32R = mybir.dt.float32r
I32 = mybir.dt.int32
ALU = mybir.AluOpType
ACT = mybir.ActivationFunctionType
AX = mybir.AxisListType.X

P = 128
DEPTH = 2
D = 1024
KT = D // P
S = 256
TT = S // P
FF = 2816
UC = 256
US = KT * UC
FJ = FF // UC
HH = 4
MH = 8
MD = 64
SW = 3 * P
EPS = 1e-6
MIN_FORGET = 1e-20
LEVELS = 9
NMASK = 8
MC = P // 2

HQ, HF, HI, HG, MQ, MK, MV, GATE = 0, 512, 1024, 1536, 2048, 2560, 3072, 3584
IN_COLS = [c + UC * i for c in (HF, HQ, MQ, MK, MV, HI, HG) for i in range(2)] + [GATE + UC * i for i in range(8)]
U_HF, U_HQ, U_MQ, U_MK, U_MV, U_HI, U_HG, U_GATE = 0, 2, 4, 6, 8, 10, 12, 14
NIN = len(IN_COLS)
U_A, U_B, U_WO = NIN, NIN + 2, NIN + 4
NMIX = NIN + 8
FFN_SLOTS = ((0, 1, 2), (1, 2, 0))
FFN_UNITS = (FJ + 1, FJ, FJ - 1)
MIX_UNITS = NMIX // 3
BASE_FFN1 = (0, 0, 0)
BASE_MIX = FFN_UNITS
BASE_FFN2 = tuple(n + MIX_UNITS for n in BASE_MIX)
PER_LAYER = tuple(BASE_FFN2[s] + FFN_UNITS[FFN_SLOTS[1].index(s)] for s in range(3))


def ffn_unit(f, l, kind, i):
    s = FFN_SLOTS[f][kind]
    return s, l * PER_LAYER[s] + (BASE_FFN1, BASE_FFN2)[f][s] + i


def mix_unit(l, u):
    s = (u + 1) % 3
    return s, l * PER_LAYER[s] + (BASE_MIX[s] + u // 3)
NORMS = 3

PR = 3 * KT + 1 + HH
C_NORM, C_HN, C_LB, C_OML, C_NOML = (0, KT, 2 * KT), 3 * KT, 3 * KT + 1, 3 * KT + 5, 3 * KT + 9
PC = 3 * KT + 13


def build(nc, x, ffn1_norm, ffn1_w_gu, ffn1_w_down, mix_norm, w_in, lb_logits, hgrn_norm, w_a, w_b, w_out,
          ffn2_norm, ffn2_w_gu, ffn2_w_down, final_norm, shape_consts, out):
    with ExitStack() as ctx:
        def sb(name, shape, dt=F32):
            return ctx.enter_context(nc.sbuf_tensor(name, shape, dt))

        def sem(name):
            return ctx.enter_context(nc.semaphore(name))

        raw = [sb(f"raw{s}", [P, US]) for s in range(3)]
        high = [sb(f"high{s}", [P, US], F32R) for s in range(3)]
        low = [sb(f"low{s}", [P, US], F32R) for s in range(3)]
        xs = sb("xs", [P, TT, D])
        xn = sb("xn", [P, TT, D])
        act_h = sb("act_h", [P, KT, S], F32R)
        act_l = sb("act_l", [P, KT, S], F32R)
        br_h = sb("br_h", [P, KT, S], F32R)
        br_l = sb("br_l", [P, KT, S], F32R)
        gates = sb("gates", [P, 2 * KT, S])
        q_sb = sb("q_sb", [P, HH * S])
        k_sb = sb("k_sb", [P, HH * S])
        f_sb = sb("f_sb", [P, HH * S])
        t_sb = sb("t_sb", [P, HH * S])
        at = sb("at", [P, 3, HH, P])
        hg_sb = sb("hg_sb", [P, TT, HH * P])
        mq_sb = sb("mq_sb", [P, HH, S])
        mk_sb = sb("mk_sb", [P, HH, S])
        s_sb = sb("s_sb", [P, 2, SW])
        pt_sb = sb("pt_sb", [P, 2, SW])
        alibi = sb("alibi", [P, MH, SW])
        ident = sb("ident", [P, P])
        consts = sb("consts", [P, SW + P + (NMASK - 1) * MC])
        fnorm = sb("fnorm", [P, D])
        rows = sb("rows", [DEPTH * PR, P])
        par = sb("par", [P, DEPTH, PC])
        cur = sb("cur", [P, PC])
        lbt = sb("lbt", [P, 6, HH])
        neg_half = sb("neg_half", [P, 2 * HH])
        ssq = sb("ssq", [P, TT, 2])
        msq = sb("msq", [P, TT])
        rstd = sb("rstd", [P, TT])
        hsq = sb("hsq", [P, 2 * HH])
        hms = sb("hms", [P, 2 * HH])
        hrs = sb("hrs", [P, 2 * HH])
        nmax = sb("nmax", [P, 2, 2])
        psums = sb("psums", [P, 2, 2])
        prec = sb("prec", [P, 2, 2])

        bank = [ctx.enter_context(nc.psum_tensor(f"bank{i}", [P, 2, S], F32)) for i in range(8)]

        distance = consts[:, 0:SW]
        diag_mask = consts[:, SW:SW + P].bitcast(I32).rearrange("p (a t) -> p a t", a=1)
        block_masks = consts[:, SW + P:].bitcast(I32).rearrange("p (m t) -> p m t", t=MC)
        inp = xn[:, 0, :].rearrange("p (t v) -> p t v", t=TT)
        val = xn[:, 1, :].rearrange("p (t v) -> p t v", t=TT)
        silu_g = gates[:, 0:2, :]
        prod = gates[:, 2:4, :]
        o_sb = t_sb[:].rearrange("p (t v) -> p t v", t=TT)
        T_BANKS = (0, 1, 6, 7)

        raw_loaded = [sem(f"raw_loaded{s}") for s in range(3)]
        high_ready = [sem(f"high_ready{s}") for s in range(3)]
        low_ready = [sem(f"low_ready{s}") for s in range(3)]
        unit_done = [sem(f"unit_done{s}") for s in range(3)]
        x_loaded = [sem(f"x_loaded{t}") for t in range(TT)]
        ident_loaded = sem("ident_loaded")
        consts_loaded = sem("consts_loaded")
        fnorm_loaded = sem("fnorm_loaded")
        rows_loaded = sem("rows_loaded")
        neg_half_set = sem("neg_half_set")
        rows_turned = sem("rows_turned")
        par_copied = sem("par_copied")
        lb_step = sem("lb_step")
        lb_diff = sem("lb_diff")
        lb_exp = sem("lb_exp")
        par_ready = sem("par_ready")
        cur_ready = sem("cur_ready")
        alibi_ready = sem("alibi_ready")
        at_zeroed = sem("at_zeroed")
        x_new = sem("x_new")
        ssq_ready = sem("ssq_ready")
        msq_ready = sem("msq_ready")
        rstd_ready = sem("rstd_ready")
        xn_ready = sem("xn_ready")
        xn_turned = sem("xn_turned")
        act_high = sem("act_high")
        act_low = sem("act_low")
        silu_ready = sem("silu_ready")
        prod_ready = sem("prod_ready")
        prod_high = sem("prod_high")
        prod_low = sem("prod_low")
        acc_done = sem("acc_done")
        evicted = sem("evicted")
        forget_raw = sem("forget_raw")
        decays_ready = sem("decays_ready")
        level_done = sem("level_done")
        level_seen = sem("level_seen")
        level_taken = sem("level_taken")
        level_t = sem("level_t")
        level_next = sem("level_next")
        o_done = sem("o_done")
        o_squared = sem("o_squared")
        o_summed = sem("o_summed")
        o_ms = sem("o_ms")
        o_rstd = sem("o_rstd")
        o_scaled = sem("o_scaled")
        hg_ready = sem("hg_ready")
        gates_ready = sem("gates_ready")
        o_gated = sem("o_gated")
        o_turned = sem("o_turned")
        o_high = sem("o_high")
        o_low = sem("o_low")
        scores_done = sem("scores_done")
        s_biased = sem("s_biased")
        s_max = sem("s_max")
        s_exp = sem("s_exp")
        s_rec = sem("s_rec")
        p_ready = sem("p_ready")
        p_turned = sem("p_turned")
        pt_ready = sem("pt_ready")
        pv_done = sem("pv_done")
        ob_high = sem("ob_high")
        ob_low = sem("ob_low")
        gated_b = sem("gated_b")
        merged = sem("merged")
        merged_high = sem("merged_high")
        merged_low = sem("merged_low")
        y_ready = sem("y_ready")
        out_stored = sem("out_stored")

        gu_v = [w.rearrange("l (k p) n -> l p k n", p=P) for w in (ffn1_w_gu, ffn2_w_gu)]
        down_v = [w.rearrange("l (j k p) n -> l j p k n", p=P, k=2) for w in (ffn1_w_down, ffn2_w_down)]
        in_v = w_in.rearrange("l (k p) n -> l p k n", p=P)
        branch_v = [w.rearrange("l (k p) n -> l p k n", p=P) for w in (w_a, w_b)]
        wo_v = w_out.rearrange("l (j k p) n -> l j p k n", p=P, k=2)

        block = ctx.enter_context(nc.Block())

        @block.sync
        def _(sp):
            def load(s, n, dst, src):
                sp.wait_ge(low_ready[s], n + 1)
                sp.dma_start(dst, src).then_inc(raw_loaded[s], 16)

            def load_gu(f, l, j, kind):
                src = gu_v[f][bass.ds(l, 1), :, :, bass.ds(j * UC + kind * FF, UC)].rearrange("l p k n -> p (l k) n")
                s, n = ffn_unit(f, l, kind, j)
                load(s, n, raw[s][:].rearrange("p (k n) -> p k n", k=KT), src)

            def load_down(f, l, j, last=False):
                src = down_v[f][bass.ds(l, 1), bass.ds(j, 1)].rearrange("l j p k n -> p (l j k) n")
                s, n = ffn_unit(f, l, 0, FJ) if last else ffn_unit(f, l, 2, j)
                load(s, n, raw[s][:].rearrange("p (k n) -> p k n", k=2), src)

            def load_mix(l, u):
                if u < NIN:
                    src = in_v[bass.ds(l, 1), :, :, IN_COLS[u]:IN_COLS[u] + UC].rearrange("l p k n -> p (l k) n")
                elif u < U_WO:
                    w, half = divmod(u - U_A, 2)
                    src = branch_v[w][bass.ds(l, 1), :, :, half * 512:half * 512 + 512].rearrange("l p k n -> p (l k) n")
                elif u < NMIX:
                    src = wo_v[bass.ds(l, 1), u - U_WO].rearrange("l p k n -> p (l k) n")
                else:
                    load_gu(1, l, 0, u - NMIX)
                    return
                s, n = mix_unit(l, u)
                load(s, n, raw[s][:].rearrange("p (k n) -> p k n", k=src.shape[1]), src)

            def ffn(f, l):
                with sp.Fori(0, FJ - 1) as j:
                    load_gu(f, l, j + 1, 0)
                    load_gu(f, l, j + 1, 1)
                    load_down(f, l, j)
                load_down(f, l, FJ - 1, last=True)
                if f == 0:
                    load_mix(l, 0)
                    load_mix(l, 1)

            for t in range(TT):
                sp.dma_start(xs[:, t, :], x[0, t * P:(t + 1) * P, :]).then_inc(x_loaded[t], 16)
            sp.wait_ge(rows_loaded, 80)
            sp.wait_ge(ident_loaded, 16)
            with sp.Fori(0, DEPTH) as l:
                load_gu(0, l, 0, 0)
                load_gu(0, l, 0, 1)
                ffn(0, l)
                for u in range(2, NMIX + 2):
                    load_mix(l, u)
                ffn(1, l)

        @block.gpsimd
        def _(pool):
            for s in range(3):
                pool.sem_inc(low_ready[s], 1)
                pool.sem_inc(unit_done[s], 1)
            pool.sem_inc(prod_low, 1)
            pool.memset(neg_half[:], -0.5).then_inc(neg_half_set, 1)
            pool.memset(at[:], 0.0).then_inc(at_zeroed, 1)
            pool.wait_ge(neg_half_set, 1)

            def norm(r):
                for t in range(TT):
                    pool.wait_ge(msq_ready, r * TT + (t + 1))
                    pool.tensor_tensor(rstd[:, t:t + 1], msq[:, t:t + 1], neg_half[:, t:t + 1],
                                       ALU.pow).then_inc(rstd_ready, 1)

            norm(0)
            pool.dma_start(consts[:], shape_consts[:, P:]).then_inc(consts_loaded, 16)
            pool.wait_ge(consts_loaded, 16)
            for h in range(MH):
                ins = pool.tensor_scalar(alibi[:, h, :], distance, 2.0 ** (-8.0 * (h + 1) / MH), None, ALU.mult)
            ins.then_inc(alibi_ready, 1)
            pool.dma_start(fnorm[:], final_norm.partition_broadcast(P)).then_inc(fnorm_loaded, 16)
            with pool.Fori(0, DEPTH) as l:
                norm(l * NORMS + 1)
                pool.wait_ge(o_ms, l + 1)
                pool.tensor_tensor(hrs[:], hms[:], neg_half[:], ALU.pow).then_inc(o_rstd, 1)
                norm(l * NORMS + 2)
                norm(l * NORMS + 3)
            for t in range(TT):
                pool.wait_ge(y_ready, t + 1)
                pool.dma_start(out[0, t * P:(t + 1) * P, :], xn[:, t, :]).then_inc(out_stored, 16)
            pool.wait_ge(out_stored, 16 * TT)

        @block.scalar
        def _(act):
            def split(s, n):
                act.wait_ge(raw_loaded[s], n * 16 + 16)
                act.wait_ge(unit_done[s], n + 1)
                act.activation(high[s][:], raw[s][:], ACT.Copy).then_inc(high_ready[s], 1)

            def square_sums(r, t):
                for n in range(2):
                    act.wait_ge(x_new, r * 4 + (2 * t + n + 1))
                    ins = act.activation(xn[:, t, 512 * n:512 * n + 512], xs[:, t, 512 * n:512 * n + 512], ACT.Square,
                                         accum_out=ssq[:, t, n:n + 1])
                ins.then_inc(ssq_ready, 1)

            def norm_high(l, i, t):
                r = l * NORMS + i
                for b in range(4):
                    act.wait_ge(xn_turned, r * 8 + (4 * t + b + 1))
                    for e in range(2):
                        kt = 2 * b + e
                        ins = act.activation(act_h[:, kt, t * P:t * P + P], bank[T_BANKS[b]][:, e, t * P:t * P + P],
                                             ACT.Copy, scale=cur[:, C_NORM[i] + kt:C_NORM[i] + kt + 1])
                    ins.then_inc(act_high, 1)

            def norm(l, i):
                for t in range(TT):
                    square_sums(l * NORMS + i, t)
                    norm_high(l, i, t)

            def ffn(f, l):
                q = (l * 2 + f) * FJ

                def silu(j):
                    s, n = ffn_unit(f, l, 0, j)
                    act.wait_ge(unit_done[s], n + 2)
                    act.activation(silu_g, bank[0][:], ACT.Silu).then_inc(silu_ready, 1)

                def product_high(j, k0=0):
                    act.wait_ge(prod_ready, q + j + 1)
                    if k0 == 0:
                        s, n = ffn_unit(f, l, 2, j)
                        act.wait_ge(unit_done[s], n + 1)
                    act.activation(br_h[:, k0:k0 + 2, :], prod, ACT.Copy).then_inc(prod_high, 1)

                with act.Fori(0, FJ - 1) as j:
                    silu(j)
                    split(*ffn_unit(f, l, 0, j + 1))
                    split(*ffn_unit(f, l, 1, j + 1))
                    product_high(j)
                    split(*ffn_unit(f, l, 2, j))
                silu(FJ - 1)
                split(*ffn_unit(f, l, 0, FJ))
                product_high(FJ - 1, 2)
                if f == 0:
                    split(*mix_unit(l, 0))

            def mixer(l):
                def evict(u):
                    s, n = mix_unit(l, u)
                    act.wait_ge(unit_done[s], n + 2)
                    src = bank[u % 2][:]
                    func, e = ACT.Copy, u % 2
                    if u < U_HQ:
                        func, dst = ACT.Sigmoid, t_sb[:, 512 * e:512 * e + 512].rearrange("p (h t) -> p h t", h=2)
                    elif u < U_MQ:
                        func, dst = ACT.Silu, q_sb[:, 512 * e:512 * e + 512].rearrange("p (h t) -> p h t", h=2)
                    elif u < U_MK:
                        dst = mq_sb[:, 2 * e:2 * e + 2, :]
                    elif u < U_MV:
                        dst = mk_sb[:, 2 * e:2 * e + 2, :]
                    elif u < U_HI:
                        dst = val[:, :, UC * e:UC * e + UC]
                    elif u < U_HG:
                        dst = inp[:, :, UC * e:UC * e + UC]
                    elif u < U_GATE:
                        dst = hg_sb[:, :, UC * e:UC * e + UC]
                    else:
                        g = u - U_GATE
                        dst = gates[:, 2 * g:2 * g + 2, :]
                        func = ACT.Copy if g < 4 else ACT.Sigmoid
                    act.activation(dst, src, func).then_inc(evicted, 1)

                def softmax_exp(h):
                    b = h % 2
                    act.wait_ge(s_max, l * MH + (h + 1))
                    act.activation(s_sb[:, b, 0:P], s_sb[:, b, 0:P], ACT.Exp, bias=nmax[:, b, 0:1],
                                   accum_out=psums[:, b, 0:1])
                    act.activation(s_sb[:, b, P:SW], s_sb[:, b, P:SW], ACT.Exp, bias=nmax[:, b, 1:2],
                                   accum_out=psums[:, b, 1:2]).then_inc(s_exp, 1)

                def probs_copy(h):
                    act.wait_ge(p_turned, l * MH + (h + 1))
                    if h >= 2:
                        act.wait_ge(pv_done, l * MH + (h - 1))
                    act.activation(pt_sb[:, h % 2, :], bank[4 + h % 2][:].rearrange("p a b -> p (a b)")[:, 0:SW],
                                   ACT.Copy).then_inc(pt_ready, 1)

                split(*mix_unit(l, 1))
                for u in range(U_B + 1):
                    split(*mix_unit(l, u + 2))
                    if u == 14:
                        act.wait_ge(o_done, l + 1)
                        for t in range(TT):
                            ins = act.activation(o_sb[:, t, :], bank[2 + t][:].rearrange("p a b -> p (a b)"),
                                                 ACT.Square)
                        ins.then_inc(o_squared, 1)
                    if 10 <= u < 10 + MH:
                        probs_copy(u - 10)
                    if u < NIN:
                        evict(u)
                    if 8 <= u < 8 + MH:
                        softmax_exp(u - 8)
                    if u == 16:
                        act.wait_ge(evicted, l * NIN + U_GATE)
                        act.activation(hg_sb[:], hg_sb[:], ACT.Silu).then_inc(hg_ready, 1)
                    if u == U_GATE + 3:
                        act.wait_ge(evicted, l * NIN + (U_GATE + 4))
                        act.activation(gates[:, 0:8, :], gates[:, 0:8, :], ACT.Sigmoid).then_inc(gates_ready, 1)
                    if u == 19:
                        for b in range(2):
                            act.wait_ge(pv_done, l * MH + 4 * (b + 1))
                            act.activation(br_h[:, 4 + 2 * b:6 + 2 * b, :], bank[6 + b][:],
                                           ACT.Copy).then_inc(ob_high, 1)
                    if u == 20:
                        act.wait_ge(o_turned, l + 1)
                        for b in range(2):
                            act.activation(br_h[:, 2 * b:2 * b + 2, :], bank[2 + b][:], ACT.Copy,
                                           scale=cur[:, C_HN:C_HN + 1]).then_inc(o_high, 1)
                for u in range(U_B + 1, NMIX - 1):
                    split(*mix_unit(l, u + 2))
                    if u < U_WO + 1:
                        half = u - U_B - 1
                        act.wait_ge(merged, l * 2 + (half + 1))
                        act.activation(act_h[:, 4 * half:4 * half + 4, :], gates[:, 4 * half:4 * half + 4, :],
                                       ACT.Copy).then_inc(merged_high, 1)

            act.dma_start(ident[:], shape_consts[:, 0:P]).then_inc(ident_loaded, 16)
            for src, row, n in ((ffn1_norm, 0, KT), (mix_norm, DEPTH * KT, KT), (ffn2_norm, 2 * DEPTH * KT, KT),
                                (hgrn_norm, 3 * DEPTH * KT, 1), (lb_logits, 3 * DEPTH * KT + DEPTH, HH)):
                act.dma_start(rows[row:row + DEPTH * n, :],
                              src.rearrange("l (k p) -> (l k) p", p=P)).then_inc(rows_loaded, 16)
            for t in range(TT):
                square_sums(0, t)
            act.wait_ge(lb_diff, 1)
            act.activation(lbt[:, 1:3, :], lbt[:, 1:3, :], ACT.Exp).then_inc(lb_exp, 1)
            with act.Fori(0, DEPTH) as l:
                split(*ffn_unit(0, l, 0, 0))
                act.wait_ge(cur_ready, l + 1)
                for t in range(TT):
                    norm_high(l, 0, t)
                split(*ffn_unit(0, l, 1, 0))
                ffn(0, l)
                norm(l, 1)
                mixer(l)
                norm(l, 2)
                split(*ffn_unit(1, l, 1, 0))
                ffn(1, l)
                for t in range(TT):
                    square_sums(l * NORMS + NORMS, t)

        @block.vector
        def _(dve):
            def split(s, n):
                dve.wait_ge(high_ready[s], n + 1)
                dve.tensor_tensor(low[s][:], raw[s][:], high[s][:].bitcast(F32),
                                  ALU.subtract).then_inc(low_ready[s], 1)

            def residual(l, i, t, scale):
                for n in range(2):
                    if t == 1 and n == 1:
                        s, last = mix_unit(l, NMIX - 1) if i == 1 else ffn_unit(i // 2, l, 0, FJ)
                        dve.wait_ge(unit_done[s], last + 2)
                    else:
                        dve.wait_ge(acc_done, l * 9 + (3 * i + 2 * t + n + 1))
                    v = xs[:, t, 512 * n:512 * n + 512]
                    dve.scalar_tensor_tensor(v, bank[2 + 2 * t + n][:].rearrange("p a b -> p (a b)"), scale, v,
                                             ALU.mult, ALU.add).then_inc(x_new, 1)

            def sum_up(r, t):
                dve.wait_ge(ssq_ready, r * TT + (t + 1))
                dve.tensor_scalar(msq[:, t:t + 1], ssq[:, t, 0:1], ssq[:, t, 1:2], D * EPS, ALU.add,
                                  ALU.add).then_inc(msq_ready, 1)

            def normalise(r, t):
                sum_up(r, t)
                dve.wait_ge(rstd_ready, r * TT + (t + 1))
                for n in range(2):
                    v = slice(512 * n, 512 * n + 512)
                    dve.tensor_scalar(xn[:, t, v], xs[:, t, v], rstd[:, t:t + 1], float(D) ** 0.5, ALU.mult,
                                      ALU.mult).then_inc(xn_ready, 1)

            def norm_low(l, i, t):
                r = l * NORMS + i
                for b in range(4):
                    dve.wait_ge(act_high, r * 8 + (4 * t + b + 1))
                    for e in range(2):
                        kt = 2 * b + e
                        v = slice(t * P, t * P + P)
                        ins = dve.scalar_tensor_tensor(act_l[:, kt, v], bank[T_BANKS[b]][:, e, v],
                                                       cur[:, C_NORM[i] + kt:C_NORM[i] + kt + 1],
                                                       act_h[:, kt, v].bitcast(F32), ALU.mult, ALU.subtract)
                    ins.then_inc(act_low, 1)

            def residual_norm(l, i, scale):
                for t in range(TT):
                    residual(l, i - 1, t, scale)
                    normalise(l * NORMS + i, t)
                    norm_low(l, i, t)

            def ffn(f, l):
                q = (l * 2 + f) * FJ

                def product(j):
                    s, n = ffn_unit(f, l, 1, j)
                    dve.wait_ge(silu_ready, q + j + 1)
                    dve.wait_ge(unit_done[s], n + 2)
                    dve.wait_ge(prod_low, q + j + 1)
                    dve.tensor_tensor(prod, bank[1][:], silu_g, ALU.mult).then_inc(prod_ready, 1)

                def product_low(j, k0=0):
                    dve.wait_ge(prod_high, q + j + 1)
                    dve.tensor_tensor(br_l[:, k0:k0 + 2, :], prod, br_h[:, k0:k0 + 2, :].bitcast(F32),
                                      ALU.subtract).then_inc(prod_low, 1)

                with dve.Fori(0, FJ - 1) as j:
                    split(*ffn_unit(f, l, 0, j + 1))
                    product(j)
                    split(*ffn_unit(f, l, 1, j + 1))
                    product_low(j)
                    split(*ffn_unit(f, l, 2, j))
                split(*ffn_unit(f, l, 0, FJ))
                product(FJ - 1)
                product_low(FJ - 1, 2)
                if f == 0:
                    split(*mix_unit(l, 0))

            def mixer(l):
                def level(i):
                    m = 1 if i == 0 else 1 << (i - 1)
                    dve.wait_ge(level_done, l * LEVELS + (i + 1))
                    dve.sem_inc(level_seen, 1)
                    if i == LEVELS - 1:
                        dve.tensor_copy(at[:, 2], bank[2][:].rearrange("p a (b t) -> p (a b) t", b=2)
                                        ).then_inc(level_taken, 1)
                        return
                    for t in range(TT):
                        if i == 0:
                            dst, mask = at[:, t], diag_mask.to_broadcast([P, HH, P])
                            src = bank[2 + t][:].rearrange("p a (b t) -> p (a b) t", b=2)
                        else:
                            dst = at[:, t].rearrange("p h (g e m) -> p h g e m", e=2, m=m)[:, :, :, 1, :]
                            mask = block_masks[:, i - 1:i, :].to_broadcast([P, HH, MC]).rearrange(
                                "p h (g m) -> p h g m", m=m)
                            src = bank[2 + t][:, 0, :].rearrange("p (h g m) -> p h g m", h=HH, m=m)
                        ins = dve.copy_predicated(dst, mask, src)
                    if i == 0:
                        dve.tensor_tensor(q_sb[:], q_sb[:], f_sb[:], ALU.mult).then_inc(level_taken, 1)
                        return
                    n = HH * S // m
                    tm = f_sb[:] if m == 1 else t_sb[:, HH * S - 2 * n:HH * S - n]
                    tb = tm.rearrange("p (g e) -> p g e", e=2)
                    qv = q_sb[:].rearrange("p (g e m) -> p g e m", e=2, m=m)
                    kv = k_sb[:].rearrange("p (g e m) -> p g e m", e=2, m=m)
                    if m > 1:
                        dve.wait_ge(level_t, l * (LEVELS - 3) + (i - 1))
                    if i < LEVELS - 2:
                        dve.tensor_tensor(t_sb[:, HH * S - n:HH * S - n // 2], tb[:, :, 0], tb[:, :, 1],
                                          ALU.mult).then_inc(level_t, 1)
                    dve.tensor_tensor(kv[:, :, 0, :], kv[:, :, 0, :], tb[:, :, 1:2].to_broadcast([P, n // 2, m]), ALU.mult)
                    dve.tensor_tensor(qv[:, :, 1, :], qv[:, :, 1, :], tb[:, :, 0:1].to_broadcast([P, n // 2, m]),
                                      ALU.mult).then_inc(level_taken, 1)

                def scores_max(h):
                    b = h % 2
                    dve.wait_ge(scores_done, l * MH + (h + 1))
                    if h >= 2:
                        dve.wait_ge(p_turned, l * MH + (h - 1))
                    dve.scalar_tensor_tensor(s_sb[:, b, :], bank[4 + b][:].rearrange("p a b -> p (a b)")[:, 0:SW],
                                             float(MD) ** -0.5, alibi[:, h, :], ALU.mult, ALU.add).then_inc(s_biased, 1)
                    dve.wait_ge(s_biased, l * MH + (h + 1))
                    dve.tensor_reduce(nmax[:, b, 0:1], s_sb[:, b, 0:P], AX, ALU.max, negate=True)
                    dve.tensor_reduce(nmax[:, b, 1:2], s_sb[:, b, P:SW], AX, ALU.max, negate=True).then_inc(s_max, 1)

                def probs_scale(h):
                    b = h % 2
                    dve.wait_ge(s_exp, l * MH + (h + 1))
                    dve.reciprocal(prec[:, b, :], psums[:, b, :]).then_inc(s_rec, 1)
                    dve.wait_ge(s_rec, l * MH + (h + 1))
                    dve.tensor_scalar(s_sb[:, b, 0:P], s_sb[:, b, 0:P], prec[:, b, 0:1], None, ALU.mult)
                    dve.tensor_scalar(s_sb[:, b, P:SW], s_sb[:, b, P:SW], prec[:, b, 1:2], None,
                                      ALU.mult).then_inc(p_ready, 1)

                def merged_split(half):
                    dve.wait_ge(merged_high, l * 2 + (half + 1))
                    dve.tensor_tensor(act_l[:, 4 * half:4 * half + 4, :], gates[:, 4 * half:4 * half + 4, :],
                                      act_h[:, 4 * half:4 * half + 4, :].bitcast(F32),
                                      ALU.subtract).then_inc(merged_low, 1)

                split(*mix_unit(l, 1))
                for u in range(NMIX - 1):
                    if u == U_B + 1:
                        merged_split(0)
                    split(*mix_unit(l, u + 2))
                    if u == 2:
                        dve.wait_ge(evicted, l * NIN + 2)
                        for h in range(HH):
                            v = slice(h * S, h * S + S)
                            oml = cur[:, C_OML + h:C_OML + h + 1]
                            ins = dve.tensor_scalar(f_sb[:, v], t_sb[:, v], oml, cur[:, C_LB + h:C_LB + h + 1],
                                                    ALU.mult, ALU.add)
                            dve.tensor_scalar(k_sb[:, v], t_sb[:, v], 1.0, cur[:, C_NOML + h:C_NOML + h + 1],
                                              ALU.subtract, ALU.mult)
                        ins.then_inc(forget_raw, 1)
                        dve.wait_ge(forget_raw, l + 1)
                        dve.tensor_scalar(f_sb[:], f_sb[:], MIN_FORGET, None, ALU.max).then_inc(decays_ready, 1)
                    if 8 <= u < 8 + MH:
                        scores_max(u - 8)
                    if 4 <= u < 4 + LEVELS:
                        if u == 4:
                            dve.wait_ge(decays_ready, l + 1)
                        level(u - 4)
                    if u == 15:
                        dve.wait_ge(o_squared, l + 1)
                        dve.tensor_reduce(hsq[:], t_sb[:].rearrange("p (g v) -> p g v", v=P), AX,
                                          ALU.add).then_inc(o_summed, 1)
                        dve.wait_ge(o_summed, l + 1)
                        dve.tensor_scalar(hms[:], hsq[:], 1.0 / P, EPS, ALU.mult, ALU.add).then_inc(o_ms, 1)
                    if u == 16:
                        dve.wait_ge(o_rstd, l + 1)
                        for t in range(TT):
                            ins = dve.tensor_tensor(o_sb[:, t, :].rearrange("p (h v) -> p h v", h=HH),
                                                    bank[2 + t][:].rearrange("p a (b v) -> p (a b) v", b=2),
                                                    hrs[:, HH * t:HH * t + HH].rearrange("p (h e) -> p h e", e=1)
                                                    .to_broadcast([P, HH, P]), ALU.mult)
                        ins.then_inc(o_scaled, 1)
                    if u == 17:
                        dve.wait_ge(o_scaled, l + 1)
                        dve.wait_ge(hg_ready, l + 1)
                        dve.tensor_tensor(o_sb[:], o_sb[:], hg_sb[:], ALU.mult).then_inc(o_gated, 1)
                    if 8 <= u < 8 + MH:
                        probs_scale(u - 8)
                    if u == 19:
                        for b in range(2):
                            dve.wait_ge(ob_high, l * 2 + (b + 1))
                            dve.tensor_tensor(br_l[:, 4 + 2 * b:6 + 2 * b, :], bank[6 + b][:],
                                              br_h[:, 4 + 2 * b:6 + 2 * b, :].bitcast(F32),
                                              ALU.subtract).then_inc(ob_low, 1)
                    if u == 20:
                        for b in range(2):
                            dve.wait_ge(o_high, l * 2 + (b + 1))
                            dve.scalar_tensor_tensor(br_l[:, 2 * b:2 * b + 2, :], bank[2 + b][:], cur[:, C_HN:C_HN + 1],
                                                     br_h[:, 2 * b:2 * b + 2, :].bitcast(F32), ALU.mult,
                                                     ALU.subtract).then_inc(o_low, 1)
                    if u in (U_A, U_A + 1):
                        half = u - U_A
                        s, n = mix_unit(l, u)
                        dve.wait_ge(unit_done[s], n + 2)
                        if half == 0:
                            dve.wait_ge(evicted, l * NIN + NIN)
                            dve.wait_ge(gates_ready, l + 1)
                        for b in range(2):
                            g = gates[:, 4 * half + 2 * b:4 * half + 2 * b + 2, :]
                            dve.tensor_tensor(g, g, bank[2 - 2 * half + b][:], ALU.mult)
                    if u in (U_B, U_B + 1):
                        half = u - U_B
                        s, n = mix_unit(l, u)
                        dve.wait_ge(unit_done[s], n + 2)
                        for b in range(2):
                            g = gates[:, KT + 4 * half + 2 * b:KT + 4 * half + 2 * b + 2, :]
                            ins = dve.tensor_tensor(g, g, bank[4 + 2 * half + b][:], ALU.mult)
                        ins.then_inc(gated_b, 1)
                        dve.wait_ge(gated_b, l * 2 + (half + 1))
                        ga = gates[:, 4 * half:4 * half + 4, :]
                        dve.tensor_tensor(ga, ga, gates[:, KT + 4 * half:KT + 4 * half + 4, :],
                                          ALU.add).then_inc(merged, 1)
                    if u == U_WO:
                        merged_split(1)

            for t in range(TT):
                dve.wait_ge(x_loaded[t], 16)
                dve.sem_inc(x_new, 2)
            for t in range(TT):
                normalise(0, t)
            dve.wait_ge(rows_turned, 1)
            pr = bank[5][:].rearrange("p a b -> p (a b)")
            for col, row, n in ((0, 0, KT), (KT, DEPTH * KT, KT), (2 * KT, 2 * DEPTH * KT, KT),
                                (C_HN, 3 * DEPTH * KT, 1), (C_LB, 3 * DEPTH * KT + DEPTH, HH)):
                ins = dve.tensor_copy(par[:, :, col:col + n],
                                      pr[:, row:row + DEPTH * n].rearrange("p (l c) -> p l c", l=DEPTH))
            ins.then_inc(par_copied, 1)
            dve.wait_ge(par_copied, 1)
            lg = par[:, :, C_LB:C_LB + HH]
            dve.tensor_tensor(lbt[:, 0, :], lg[:, 0], lg[:, 1], ALU.max).then_inc(lb_step, 1)
            dve.wait_ge(lb_step, 1)
            for i in range(DEPTH):
                ins = dve.tensor_tensor(lbt[:, 1 + i, :], lg[:, i], lbt[:, 0, :], ALU.subtract)
            ins.then_inc(lb_diff, 1)
            dve.wait_ge(lb_exp, 1)
            dve.tensor_tensor(lbt[:, 3, :], lbt[:, 1, :], lbt[:, 2, :], ALU.add).then_inc(lb_step, 1)
            dve.wait_ge(lb_step, 2)
            dve.reciprocal(lbt[:, 0, :], lbt[:, 3, :]).then_inc(lb_step, 1)
            dve.wait_ge(lb_step, 3)
            for i in range(DEPTH):
                ins = dve.tensor_tensor(lbt[:, 4 + i, :], lbt[:, 1 + i, :], lbt[:, 0, :], ALU.mult)
            ins.then_inc(lb_step, 1)
            dve.wait_ge(lb_step, 4)
            dve.tensor_tensor(lbt[:, 3, :], lbt[:, 4, :], lbt[:, 5, :], ALU.add).then_inc(lb_step, 1)
            dve.wait_ge(lb_step, 5)
            dve.tensor_tensor(lg[:, 0], lbt[:, 4, :], lbt[:, 4, :], ALU.subtract)
            dve.tensor_tensor(lg[:, 1], lbt[:, 3, :], lbt[:, 4, :], ALU.subtract).then_inc(lb_step, 1)
            dve.wait_ge(lb_step, 6)
            dve.tensor_scalar(lg, lg, 0.0, 1.0, ALU.max, ALU.min).then_inc(lb_step, 1)
            dve.wait_ge(lb_step, 7)
            dve.tensor_scalar(par[:, :, C_OML:C_OML + HH], lg, -1.0, 1.0, ALU.mult, ALU.add)
            dve.tensor_scalar(par[:, :, C_NOML:C_NOML + HH], lg, 1.0, None, ALU.subtract).then_inc(par_ready, 1)
            dve.wait_ge(par_ready, 1)
            with dve.Fori(0, DEPTH) as l:
                dve.tensor_copy(cur[:], par[:, bass.ds(l, 1), :].rearrange("p l c -> p (l c)")).then_inc(cur_ready, 1)
                split(*ffn_unit(0, l, 0, 0))
                dve.wait_ge(cur_ready, l + 1)
                for t in range(TT):
                    norm_low(l, 0, t)
                split(*ffn_unit(0, l, 1, 0))
                ffn(0, l)
                residual_norm(l, 1, 0.5)
                mixer(l)
                residual_norm(l, 2, 1.0)
                split(*ffn_unit(1, l, 1, 0))
                ffn(1, l)
                for t in range(TT):
                    residual(l, 2, t, 0.5)
                    normalise(l * NORMS + NORMS, t)
            dve.wait_ge(fnorm_loaded, 16)
            for t in range(TT):
                dve.wait_ge(xn_ready, (DEPTH * NORMS * TT + t + 1) * 2)
                dve.tensor_tensor(xn[:, t, :], xn[:, t, :], fnorm[:], ALU.mult).then_inc(y_ready, 1)

        @block.tensor
        def _(pe):
            def products(dst, left, right, first, last):
                pe.matmul(dst, left[0], right[0], start=first, stop=False)
                pe.matmul(dst, left[0], right[1], start=False, stop=False)
                return pe.matmul(dst, left[1], right[0], start=False, stop=last)

            def act_pair(k, cols):
                return act_h[:, k, cols], act_l[:, k, cols]

            def br_pair(k, cols):
                return br_h[:, k, cols], br_l[:, k, cols]

            def w_pair(s, start, n):
                return high[s][:, start:start + n], low[s][:, start:start + n]

            def cols(t):
                return slice(t * P, t * P + P)

            ALL = slice(0, S)

            def norm_turns(r, t):
                for b in range(4):
                    if b % 2 == 0:
                        pe.wait_ge(xn_ready, r * 4 + (2 * t + b // 2 + 1))
                    if t == 1:
                        pe.wait_ge(act_low, r * 8 + (b + 1))
                    for e in range(2):
                        kt = 2 * b + e
                        ins = pe.transpose(bank[T_BANKS[b]][:, e, cols(t)], xn[:, t, kt * P:kt * P + P], ident[:])
                    ins.then_inc(xn_turned, 1)

            def wide_unit(s, n, dst, norm=None, token_major=False):
                pe.wait_ge(low_ready[s], n + 2)
                for g in range(2):
                    for k in range(KT):
                        if norm is not None and g == 0 and k % 2 == 0:
                            pe.wait_ge(act_low, norm * 8 + (4 + k // 2 + 1))
                        if token_major:
                            ins = products(dst[:, g, :], act_pair(k, cols(g)), w_pair(s, k * UC, UC), k == 0, k == KT - 1)
                        else:
                            ins = products(dst[:, g, :], w_pair(s, k * UC + g * P, P), act_pair(k, ALL), k == 0,
                                           k == KT - 1)
                ins.then_inc(unit_done[s], 1)

            def residual_quarter(s, pair, k0, t, h, first, last):
                for e in range(2):
                    ins = products(bank[2 + 2 * t + h][:].rearrange("p a b -> p (a b)"), pair(k0 + e, cols(t)),
                                   w_pair(s, e * D + h * 512, 512), first and e == 0, last and e == 1)
                return ins

            def residual_unit(s, n, pair, k0, first):
                pe.wait_ge(low_ready[s], n + 2)
                for t in range(TT):
                    for h in range(2):
                        ins = residual_quarter(s, pair, k0, t, h, first, False)
                ins.then_inc(unit_done[s], 1)

            def residual_tail(a, b, pair, ka, kb, norm=None):
                for h in range(2):
                    residual_quarter(b[0], pair, kb, 0, h, False, True).then_inc(acc_done, 1)
                for h in range(2):
                    ins = residual_quarter(a[0], pair, ka, 1, h, False, False)
                ins.then_inc(unit_done[a[0]], 1)
                residual_quarter(b[0], pair, kb, 1, 0, False, True).then_inc(acc_done, 1)
                if norm is not None:
                    norm_turns(norm, 0)
                residual_quarter(b[0], pair, kb, 1, 1, False, True).then_inc(unit_done[b[0]], 1)
                if norm is not None:
                    norm_turns(norm, 1)

            def ffn(f, l):
                q = (l * 2 + f) * FJ

                def gate(j, norm=None):
                    if norm is None:
                        pe.wait_ge(silu_ready, q + j)
                    wide_unit(*ffn_unit(f, l, 0, j), bank[0], norm)

                def up(j, first=False):
                    if not first:
                        pe.wait_ge(prod_ready, q + j)
                    wide_unit(*ffn_unit(f, l, 1, j), bank[1])

                def down(j, first=False):
                    pe.wait_ge(prod_low, q + j + 2)
                    residual_unit(*ffn_unit(f, l, 2, j), br_pair, 0, first)

                gate(0, l * NORMS + 2 * f)
                up(0, True)
                gate(1)
                up(1)
                down(0, first=True)
                with pe.Fori(2, FJ - 1) as j:
                    gate(j)
                    up(j)
                    down(j - 1)
                gate(FJ - 1)
                up(FJ - 1)
                pe.wait_ge(prod_low, q + FJ)
                a, b = ffn_unit(f, l, 2, FJ - 2), ffn_unit(f, l, 0, FJ)
                pe.wait_ge(low_ready[a[0]], a[1] + 2)
                for h in range(2):
                    residual_quarter(a[0], br_pair, 0, 0, h, False, False)
                pe.wait_ge(prod_low, q + FJ + 1)
                pe.wait_ge(low_ready[b[0]], b[1] + 2)
                residual_tail(a, b, br_pair, 0, 2, l * NORMS + 1 if f == 0 else None)

            def mixer(l):
                def level(i):
                    if i == 0:
                        pe.wait_ge(evicted, l * NIN + U_MQ)
                        pe.wait_ge(decays_ready, l + 1)
                    else:
                        pe.wait_ge(level_taken, l * LEVELS + i)
                    if i == LEVELS - 1:
                        for h in range(HH):
                            ins = pe.matmul(bank[2][:, h // 2, cols(h % 2)], k_sb[:, h * S:h * S + P],
                                            q_sb[:, h * S + P:h * S + S], start=True, stop=True)
                    else:
                        for t in range(TT):
                            for h in range(HH):
                                v = slice(h * S + t * P, h * S + t * P + P)
                                if i == 0:
                                    dst, q = bank[2 + t][:, h // 2, cols(h % 2)], q_sb[:, v]
                                else:
                                    m = 1 << (i - 1)
                                    dst = bank[2 + t][:, 0, h * MC:h * MC + MC]
                                    q = q_sb[:, v].rearrange("p (g e m) -> p g e m", e=2, m=m)[:, :, 1, :]
                                ins = pe.matmul(dst, k_sb[:, v], q, start=True, stop=True)
                    ins.then_inc(level_done, 1)

                def hgrn_out():
                    pe.wait_ge(level_taken, l * LEVELS + LEVELS)
                    pe.wait_ge(evicted, l * NIN + U_HG)
                    for h in range(HH):
                        v = slice(h * P, h * P + P)
                        pe.matmul(bank[2][:, h // 2, cols(h % 2)], at[:, 0, h, :], inp[:, 0, v], start=True, stop=True)
                    for h in range(HH):
                        v = slice(h * P, h * P + P)
                        pe.matmul(bank[3][:, h // 2, cols(h % 2)], at[:, 2, h, :], inp[:, 0, v], start=True, stop=False)
                        ins = pe.matmul(bank[3][:, h // 2, cols(h % 2)], at[:, 1, h, :], inp[:, 1, v], start=False,
                                        stop=True)
                    ins.then_inc(o_done, 1)

                def hgrn_turns():
                    pe.wait_ge(o_gated, l + 1)
                    for h in range(HH):
                        for t in range(TT):
                            ins = pe.transpose(bank[2 + h // 2][:, h % 2, cols(t)], o_sb[:, t, h * P:h * P + P], ident[:])
                    ins.then_inc(o_turned, 1)

                def scores(h):
                    if h == 0:
                        pe.wait_ge(evicted, l * NIN + U_MV)
                    if h >= 2:
                        pe.wait_ge(pt_ready, l * MH + (h - 1))
                    v = slice(MD * (h % 2), MD * (h % 2) + MD)
                    b = bank[4 + h % 2][:].rearrange("p a b -> p (a b)")
                    pe.matmul(b[:, 0:P], mq_sb[v, h // 2, 0:P], mk_sb[v, h // 2, 0:P], start=True, stop=True)
                    pe.matmul(b[:, P:SW], mq_sb[v, h // 2, P:S], mk_sb[v, h // 2, :], start=True,
                              stop=True).then_inc(scores_done, 1)

                def probs_turns(h):
                    pe.wait_ge(p_ready, l * MH + (h + 1))
                    b = bank[4 + h % 2][:].rearrange("p a b -> p (a b)")
                    for c in range(3):
                        ins = pe.transpose(b[:, cols(c)], s_sb[:, h % 2, cols(c)], ident[:])
                    ins.then_inc(p_turned, 1)

                def values(h):
                    if h == 0:
                        pe.wait_ge(evicted, l * NIN + U_HI)
                    pe.wait_ge(pt_ready, l * MH + (h + 1))
                    dst = bank[6 + h // 4][MD * (h % 2):MD * (h % 2) + MD, (h // 2) % 2, :]
                    v = slice(MD * h, MD * h + MD)
                    pe.matmul(dst, val[:, 0, v], pt_sb[:, h % 2, 0:S], start=True, stop=False)
                    pe.matmul(dst[:, P:S], val[:, 1, v], pt_sb[:, h % 2, S:SW], start=False,
                              stop=True).then_inc(pv_done, 1)

                for u in range(NMIX - 1):
                    s, n = mix_unit(l, u)
                    if u < NIN:
                        if u >= 2:
                            pe.wait_ge(evicted, l * NIN + (u - 1))
                        wide_unit(s, n, bank[u % 2], l * NORMS + 1 if u == 0 else None,
                                  U_MV <= u < U_GATE)
                    elif u < U_WO:
                        half = (u - U_A) % 2
                        if u == U_A:
                            pe.wait_ge(o_low, l * 2 + 2)
                        if u == U_A + 1:
                            pe.wait_ge(evicted, l * NIN + NIN)
                        if u == U_B:
                            pe.wait_ge(ob_low, l * 2 + 2)
                        pe.wait_ge(low_ready[s], n + 2)
                        b0, k0 = (2 - 2 * half, 0) if u < U_B else (4 + 2 * half, 4)
                        for m in range(4):
                            for k in range(4):
                                ins = products(bank[b0 + m // 2][:, m % 2, :], w_pair(s, k * 512 + m * P, P),
                                               br_pair(k0 + k, ALL), k == 0, k == 3)
                        ins.then_inc(unit_done[s], 1)
                    else:
                        i = u - U_WO
                        if i % 2 == 0:
                            pe.wait_ge(merged_low, l * 2 + (i // 2 + 1))
                        if i < 2:
                            residual_unit(s, n, act_pair, 2 * i, i == 0)
                        else:
                            b = mix_unit(l, u + 1)
                            pe.wait_ge(low_ready[s], n + 2)
                            for h in range(2):
                                residual_quarter(s, act_pair, 4, 0, h, False, False)
                            pe.wait_ge(low_ready[b[0]], b[1] + 2)
                            residual_tail((s, n), b, act_pair, 4, 6, l * NORMS + 2)
                    if 10 <= u < 10 + MH:
                        values(u - 10)
                    if 9 <= u < 9 + MH:
                        probs_turns(u - 9)
                    if 8 <= u < 8 + MH:
                        scores(u - 8)
                    if 4 <= u < 4 + LEVELS:
                        level(u - 4)
                    if u == 13:
                        hgrn_out()
                    if u == 19:
                        hgrn_turns()

            pe.wait_ge(rows_loaded, 80)
            pe.wait_ge(ident_loaded, 16)
            pe.transpose(bank[5][:].rearrange("p a b -> p (a b)")[:, 0:DEPTH * PR], rows[:],
                         ident[0:DEPTH * PR, 0:DEPTH * PR]).then_inc(rows_turned, 1)
            with pe.Fori(0, DEPTH) as l:
                for t in range(TT):
                    norm_turns(l * NORMS, t)
                ffn(0, l)
                mixer(l)
                ffn(1, l)


_INS = ['x', 'ffn1_norm', 'ffn1_w_gu', 'ffn1_w_down', 'mix_norm', 'w_in', 'hgrn_lb_logits', 'hgrn_norm', 'w_branch_a',
        'w_branch_b', 'w_out', 'ffn2_norm', 'ffn2_w_gu', 'ffn2_w_down', 'final_norm']


def kernel(**inputs):
    import numpy as _np
    import concourse.bacc as _bacc
    from concourse.bass_utils import run_bass_kernel_spmd as _run

    nc = _bacc.Bacc("TRN2", target_bir_lowering=False, num_devices=1)
    arrays, args = {}, []
    for name in _INS:
        a = _np.ascontiguousarray(inputs[name])
        arrays[f"in_{name}"] = a
        args.append(nc.dram_tensor(f"in_{name}", a.shape, mybir.dt.from_np(a.dtype), kind="ExternalInput").ap())
    key, query = _np.arange(P)[None, :], _np.arange(P)[:, None]
    same = key - query
    causal = _np.where(same <= 0, same, -4e11)
    src, dst = query, key
    masks = [src == dst]
    for i in range(NMASK - 1):
        m = 1 << i
        mask = (src // (2 * m) == dst // (2 * m)) & (src // m % 2 == 0)
        masks.append(mask[:, _np.arange(P) // m % 2 == 1])
    consts = _np.concatenate([_np.eye(P), causal, same - P, causal] + masks, axis=1).astype(_np.float32)
    arrays["shape_consts"] = consts
    args.append(nc.dram_tensor("shape_consts", consts.shape, F32, kind="ExternalInput").ap())
    args.append(nc.dram_tensor("out_0", (1, S, D), F32, kind="ExternalOutput").ap())
    build(nc, *args)
    r = _run(nc, [arrays], core_ids=[0])
    return r.results[0]["out_0"]
```

```python
from contextlib import ExitStack

import concourse.bass as bass
from concourse import mybir

F32 = mybir.dt.float32
F32R = mybir.dt.float32r
I32 = mybir.dt.int32
ALU = mybir.AluOpType
ACT = mybir.ActivationFunctionType
AX = mybir.AxisListType.X

P = 128
DEPTH = 2
D = 1024
KT = D // P
S = 256
TT = S // P
FF = 2816
UC = 256
US = KT * UC
FJ = FF // UC
HH = 4
MH = 8
MD = 64
SW = 3 * P
EPS = 1e-6
MIN_FORGET = 1e-20
LEVELS = 9
NMASK = 8
MC = P // 2

HQ, HF, HI, HG, MQ, MK, MV, GATE = 0, 512, 1024, 1536, 2048, 2560, 3072, 3584
IN_UNITS = [(HI, 0), (HF, 0), (HF, 1), (HQ, 0), (HQ, 1), (MQ, 0), (MQ, 1), (MK, 0), (MK, 1), (MV, 0), (MV, 1), (HI, 1),
            (HG, 0), (HG, 1)] + [(GATE, i) for i in range(8)]
NIN = len(IN_UNITS)
TOKEN_MAJOR = (HI, MV, HG)


def taken(col):
    return max(u for u, (c, _) in enumerate(IN_UNITS) if c == col) + 1


U_GATE = IN_UNITS.index((GATE, 0))
U_LEVEL = taken(HQ)
U_OUT = U_LEVEL + LEVELS
U_SCORES = taken(MK)
U_RAW = U_SCORES + MH
U_A, U_B, U_WO = NIN, NIN + 2, NIN + 4
NMIX = NIN + 8
MIX_UNITS = NMIX // 3
PER_LAYER = 2 * FJ + MIX_UNITS


def ffn_unit(f, l, kind, i):
    base = l * PER_LAYER + (0, FJ + MIX_UNITS)[f]
    if kind < 2 and isinstance(i, int) and i == 0:
        return kind, base
    if kind == 2 and isinstance(i, int) and i == FJ - 1:
        return 2, base + FJ - 1
    return ((2, base + i - 1), (0, base + i), (1, base + i + 1))[kind]


def mix_unit(l, u):
    return u % 3, l * PER_LAYER + (FJ + u // 3)


def same_kind(u):
    kinds = [c in TOKEN_MAJOR for c, _ in IN_UNITS]
    return kinds[:u + 1].count(kinds[u])


NTOKEN = sum(c in TOKEN_MAJOR for c, _ in IN_UNITS)
NORMS = 3

PR = 3 * KT + 1 + HH
C_NORM, C_HN = (0, KT, 2 * KT), 3 * KT
C_LB, C_OML, C_NOML = 0, HH, 2 * HH


def build(nc, x, ffn1_norm, ffn1_w_gu, ffn1_w_down, mix_norm, w_in, lb_logits, hgrn_norm, w_a, w_b, w_out,
          ffn2_norm, ffn2_w_gu, ffn2_w_down, final_norm, shape_consts, out):
    with ExitStack() as ctx:
        def sb(name, shape, dt=F32):
            return ctx.enter_context(nc.sbuf_tensor(name, shape, dt))

        def sem(name):
            return ctx.enter_context(nc.semaphore(name))

        raw = [sb(f"raw{s}", [P, US]) for s in range(3)]
        high = [sb(f"high{s}", [P, US], F32R) for s in range(3)]
        low = [sb(f"low{s}", [P, US], F32R) for s in range(3)]
        xs = sb("xs", [P, TT, D])
        xn = sb("xn", [P, TT, D])
        act_h = sb("act_h", [P, KT, S], F32R)
        act_l = sb("act_l", [P, KT, S], F32R)
        br_h = sb("br_h", [P, KT, S], F32R)
        br_l = sb("br_l", [P, KT, S], F32R)
        gates = sb("gates", [P, 2 * KT, S])
        q_sb = sb("q_sb", [P, HH * S])
        k_sb = sb("k_sb", [P, HH * S])
        f_sb = sb("f_sb", [P, HH * S])
        t_sb = sb("t_sb", [P, HH * S])
        at = sb("at", [P, 3, HH, P])
        hg_sb = sb("hg_sb", [P, TT, HH * P])
        mq_sb = sb("mq_sb", [P, HH, S])
        mk_sb = sb("mk_sb", [P, HH, S])
        s_sb = sb("s_sb", [P, 2, SW])
        pt_sb = sb("pt_sb", [P, 2, SW])
        alibi = sb("alibi", [P, MH, SW])
        ident = sb("ident", [P, P])
        consts = sb("consts", [P, SW + P + (NMASK - 1) * MC])
        fnorm = sb("fnorm", [P, D])
        rows = sb("rows", [DEPTH * PR, P])
        first_rows = sb("first_rows", [KT, P])
        par = sb("par", [P, DEPTH, C_HN + 1])
        cur = sb("cur", [P, C_HN + 1])
        bounds = sb("bounds", [P, DEPTH, 3 * HH])
        cur_lb = sb("cur_lb", [P, 3 * HH])
        lbt = sb("lbt", [P, DEPTH + 1, HH])
        lbp = sb("lbp", [P, 4, DEPTH, HH])
        table = sb("table", [P, 1])
        neg_half = sb("neg_half", [P, 2 * HH])
        ssq = sb("ssq", [P, TT, 2])
        msq = sb("msq", [P, TT])
        rstd = sb("rstd", [P, TT])
        scale_t = sb("scale_t", [P, TT])
        half_scale = sb("half_scale", [P, TT])
        diag = sb("diag", [P, TT, P])
        ones = sb("ones", [P, P])
        scale_f = sb("scale_f", [P, S])
        hsq = sb("hsq", [P, 2 * HH])
        hms = sb("hms", [P, 2 * HH])
        hrs = sb("hrs", [P, 2 * HH])
        nmax = sb("nmax", [P, 2, 2])
        psums = sb("psums", [P, 2, 2])
        prec = sb("prec", [P, 2, 2])

        bank = [ctx.enter_context(nc.psum_tensor(f"bank{i}", [P, 2, S], F32)) for i in range(8)]

        distance = consts[:, 0:SW]
        diag_mask = consts[:, SW:SW + P].bitcast(I32).rearrange("p (a t) -> p a t", a=1)
        block_masks = consts[:, SW + P:].bitcast(I32).rearrange("p (m t) -> p m t", t=MC)
        inp = xn[:, 0, :].rearrange("p (t v) -> p t v", t=TT)
        val = xn[:, 1, :].rearrange("p (t v) -> p t v", t=TT)
        silu_g = gates[:, 0:2, :]
        prod = gates[:, 2:4, :]
        gate_in = gates[:, 4:6, :]
        squares = [gates[:, 6 + 2 * i:8 + 2 * i, :].rearrange("p a b -> p (a b)") for i in range(2 * TT)]
        o_sb = t_sb[:].rearrange("p (t v) -> p t v", t=TT)
        T_BANKS = (6, 7, 2, 3)

        raw_loaded = [sem(f"raw_loaded{s}") for s in range(3)]
        high_ready = [sem(f"high_ready{s}") for s in range(3)]
        half_loaded = [sem(f"half_loaded{s}") for s in range(2)]
        half_high = [sem(f"half_high{s}") for s in range(2)]
        half_low = sem("half_low")
        low_ready = [sem(f"low_ready{s}") for s in range(3)]
        unit_done = [sem(f"unit_done{s}") for s in range(3)]
        x_loaded = [sem(f"x_loaded{t}") for t in range(TT)]
        ident_loaded = sem("ident_loaded")
        consts_loaded = sem("consts_loaded")
        fnorm_loaded = sem("fnorm_loaded")
        fnorm_scaled = sem("fnorm_scaled")
        rows_loaded = sem("rows_loaded")
        neg_half_set = sem("neg_half_set")
        rows_turned = sem("rows_turned")
        par_copied = sem("par_copied")
        lb_step = sem("lb_step")
        lb_diff = sem("lb_diff")
        lb_set = sem("lb_set")
        lb_done = sem("lb_done")
        bounds_ready = sem("bounds_ready")
        first_rows_loaded = sem("first_rows_loaded")
        first_rows_turned = sem("first_rows_turned")
        first_cur_ready = sem("first_cur_ready")
        cur_ready = sem("cur_ready")
        cur_lb_ready = sem("cur_lb_ready")
        table_loaded = sem("table_loaded")
        alibi_ready = sem("alibi_ready")
        at_zeroed = sem("at_zeroed")
        x_new = sem("x_new")
        ssq_ready = sem("ssq_ready")
        msq_ready = sem("msq_ready")
        rstd_ready = sem("rstd_ready")
        scale_ready = sem("scale_ready")
        scale_spread = sem("scale_spread")
        scale_f_ready = sem("scale_f_ready")
        ones_set = sem("ones_set")
        x_turned = sem("x_turned")
        act_high = sem("act_high")
        act_low = sem("act_low")
        gate_scaled = sem("gate_scaled")
        silu_ready = sem("silu_ready")
        prod_ready = sem("prod_ready")
        prod_high = sem("prod_high")
        prod_low = sem("prod_low")
        acc_done = sem("acc_done")
        evicted_t = sem("evicted_t")
        evicted_f = sem("evicted_f")
        f_squashed = sem("f_squashed")
        q_squashed = sem("q_squashed")
        forget_raw = sem("forget_raw")
        decays_ready = sem("decays_ready")
        level_done = sem("level_done")
        level_seen = sem("level_seen")
        level_taken = sem("level_taken")
        level_t = sem("level_t")
        o_done = sem("o_done")
        o_squared = sem("o_squared")
        o_summed = sem("o_summed")
        o_ms = sem("o_ms")
        o_rstd = sem("o_rstd")
        o_scaled = sem("o_scaled")
        hg_ready = sem("hg_ready")
        gates_ready = sem("gates_ready")
        o_gated = sem("o_gated")
        o_turned = sem("o_turned")
        o_high = sem("o_high")
        o_low = sem("o_low")
        scores_done = sem("scores_done")
        s_biased = sem("s_biased")
        s_max = sem("s_max")
        s_exp = sem("s_exp")
        s_rec = sem("s_rec")
        p_ready = sem("p_ready")
        p_turned = sem("p_turned")
        pt_ready = sem("pt_ready")
        pv_done = sem("pv_done")
        ob_high = sem("ob_high")
        ob_low = sem("ob_low")
        gated_b = sem("gated_b")
        merged = sem("merged")
        merged_high = sem("merged_high")
        merged_low = sem("merged_low")
        weights_done = sem("weights_done")
        y_ready = [sem(f"y_ready{n}") for n in range(2)]
        out_stored = sem("out_stored")

        gu_v = [w.rearrange("l (k p) n -> l p k n", p=P) for w in (ffn1_w_gu, ffn2_w_gu)]
        down_v = [w.rearrange("l (j k p) n -> l j p k n", p=P, k=2) for w in (ffn1_w_down, ffn2_w_down)]
        in_v = w_in.rearrange("l (k p) n -> l p k n", p=P)
        branch_v = [w.rearrange("l (k p) n -> l p k n", p=P) for w in (w_a, w_b)]
        wo_v = w_out.rearrange("l (j k p) n -> l j p k n", p=P, k=2)

        def wait_evicted(engine, l, u):
            if IN_UNITS[u][0] in TOKEN_MAJOR:
                engine.wait_ge(evicted_t, l * NTOKEN + same_kind(u))
            else:
                engine.wait_ge(evicted_f, l * (NIN - NTOKEN) + same_kind(u))

        block = ctx.enter_context(nc.Block())

        @block.sync
        def _(sp):
            def load(s, n, dst, src):
                sp.wait_ge(low_ready[s], n + 1)
                sp.dma_start(dst, src).then_inc(raw_loaded[s], 16)

            def load_gu(f, l, j, kind):
                src = gu_v[f][bass.ds(l, 1), :, :, bass.ds(j * UC + kind * FF, UC)].rearrange("l p k n -> p (l k) n")
                s, n = ffn_unit(f, l, kind, j)
                load(s, n, raw[s][:].rearrange("p (k n) -> p k n", k=KT), src)

            def load_down(f, l, j):
                src = down_v[f][bass.ds(l, 1), bass.ds(j, 1)].rearrange("l j p k n -> p (l j k) n")
                s, n = ffn_unit(f, l, 2, j)
                load(s, n, raw[s][:].rearrange("p (k n) -> p k n", k=2), src)

            def load_mix(l, u):
                if u < NIN:
                    col, part = IN_UNITS[u]
                    src = in_v[bass.ds(l, 1), :, :, col + part * UC:col + part * UC + UC].rearrange("l p k n -> p (l k) n")
                elif u < U_WO:
                    w, half = divmod(u - U_A, 2)
                    src = branch_v[w][bass.ds(l, 1), :, :, half * 512:half * 512 + 512].rearrange("l p k n -> p (l k) n")
                elif u < NMIX:
                    src = wo_v[bass.ds(l, 1), u - U_WO].rearrange("l p k n -> p (l k) n")
                else:
                    load_gu(1, l, 0, u - NMIX)
                    return
                s, n = mix_unit(l, u)
                load(s, n, raw[s][:].rearrange("p (k n) -> p k n", k=src.shape[1]), src)

            def ffn(f, l):
                with sp.Fori(0, FJ - 1) as j:
                    load_gu(f, l, j + 1, 0)
                    load_gu(f, l, j + 1, 1)
                    load_down(f, l, j)
                load_down(f, l, FJ - 1)

            def layer(l):
                ffn(0, l)
                for u in range(NMIX + 2):
                    load_mix(l, u)
                ffn(1, l)

            sp.dma_start(xs[:, 0, :], x[0, 0:P, :]).then_inc(x_loaded[0], 16)
            sp.dma_start(ident[:], shape_consts[:, 0:P]).then_inc(ident_loaded, 16)
            sp.dma_start(first_rows[:], ffn1_norm[0].rearrange("(k p) -> k p", p=P)).then_inc(first_rows_loaded, 16)
            sp.dma_start(xs[:, 1, :], x[0, P:2 * P, :]).then_inc(x_loaded[1], 16)
            for s in range(2):
                src = gu_v[0][0, :, :, s * FF:s * FF + UC]
                for half, loaded in enumerate((half_loaded[s], raw_loaded[s])):
                    ks = slice(KT // 2 * half, KT // 2 * (half + 1))
                    sp.dma_start(raw[s][:].rearrange("p (k n) -> p k n", k=KT)[:, ks], src[:, ks]).then_inc(loaded, 16)
            for src, row, n in ((ffn1_norm, 0, KT), (mix_norm, DEPTH * KT, KT), (ffn2_norm, 2 * DEPTH * KT, KT),
                                (hgrn_norm, 3 * DEPTH * KT, 1), (lb_logits, 3 * DEPTH * KT + DEPTH, HH)):
                sp.dma_start(rows[row:row + DEPTH * n, :],
                             src.rearrange("l (k p) -> (l k) p", p=P)).then_inc(rows_loaded, 16)
            with sp.Fori(0, DEPTH - 1) as l:
                layer(l)
                load_gu(0, l + 1, 0, 0)
                load_gu(0, l + 1, 0, 1)
            layer(DEPTH - 1)
            for i in range(2 * TT):
                t, v = i // 2, slice(512 * (i % 2), 512 * (i % 2) + 512)
                sp.wait_ge(y_ready[i % 2], t + 1)
                sp.dma_start(out[0, t * P:(t + 1) * P, v], xn[:, t, v]).then_inc(out_stored, 16)
            sp.wait_ge(out_stored, 32 * TT)

        @block.gpsimd
        def _(pool):
            for s in range(3):
                pool.sem_inc(low_ready[s], 1)
                pool.sem_inc(unit_done[s], 1)
            pool.sem_inc(prod_low, 1)
            pool.memset(neg_half[:], -0.5).then_inc(neg_half_set, 1)
            pool.memset(at[:], 0.0).then_inc(at_zeroed, 1)
            pool.memset(ones[:], 1.0).then_inc(ones_set, 1)
            pool.wait_ge(neg_half_set, 1)

            def norm(r):
                for t in range(TT):
                    pool.wait_ge(msq_ready, r * TT + (t + 1))
                    pool.tensor_tensor(rstd[:, t:t + 1], msq[:, t:t + 1], neg_half[:, t:t + 1],
                                       ALU.pow).then_inc(rstd_ready, 1)

            for t in range(TT):
                pool.wait_ge(x_loaded[t], 16)
                pool.sem_inc(x_new, 2)
            norm(0)
            for ref, value in ((2, 2.718281828459045), (3, -1.0)):
                pool.memset(lbp[:, ref, :, :], value).then_inc(lb_set, 1)
            pool.wait_ge(lb_set, 2)
            pool.wait_ge(lb_diff, 1)
            pool.tensor_tensor(lbp[:, 0, :, :], lbp[:, 2, :, :], lbt[:, 0:DEPTH, :], ALU.pow).then_inc(lb_done, 1)
            pool.wait_ge(lb_done, 1)
            pool.tensor_tensor(lbp[:, 1, 0, :], lbp[:, 0, 0, :], lbp[:, 0, 1, :], ALU.add).then_inc(lb_done, 1)
            pool.wait_ge(lb_done, 2)
            pool.tensor_tensor(lbp[:, 1, 1, :], lbp[:, 1, 0, :], lbp[:, 3, 0, :], ALU.pow).then_inc(lb_done, 1)
            pool.wait_ge(lb_done, 3)
            for i in range(DEPTH):
                ins = pool.tensor_tensor(lbp[:, 0, i, :], lbp[:, 0, i, :], lbp[:, 1, 1, :], ALU.mult)
            ins.then_inc(lb_done, 1)
            pool.wait_ge(lb_done, 4)
            pool.tensor_tensor(lbp[:, 1, 0, :], lbp[:, 0, 0, :], lbp[:, 0, 1, :], ALU.add).then_inc(lb_done, 1)
            pool.wait_ge(lb_done, 5)
            pool.tensor_tensor(lbp[:, 1, 1, :], lbp[:, 1, 0, :], lbp[:, 0, 0, :], ALU.subtract)
            pool.tensor_tensor(lbp[:, 2, 0, :], lbp[:, 0, 0, :], lbp[:, 0, 0, :], ALU.subtract).then_inc(lb_done, 1)
            pool.wait_ge(lb_done, 6)
            for l, src in ((0, lbp[:, 2, 0, :]), (1, lbp[:, 1, 1, :])):
                ins = pool.tensor_scalar(bounds[:, l, C_LB:C_LB + HH], src, 0.0, 1.0, ALU.max, ALU.min)
            ins.then_inc(lb_done, 1)
            pool.wait_ge(lb_done, 7)
            lb = bounds[:, :, C_LB:C_LB + HH]
            pool.tensor_scalar(bounds[:, :, C_OML:C_OML + HH], lb, -1.0, 1.0, ALU.mult, ALU.add)
            pool.tensor_scalar(bounds[:, :, C_NOML:C_NOML + HH], lb, 1.0, None, ALU.subtract).then_inc(bounds_ready, 1)
            pool.wait_ge(rows_loaded, 80)
            pool.dma_start(consts[:], shape_consts[:, P:]).then_inc(consts_loaded, 16)
            pool.wait_ge(consts_loaded, 16)
            for h in range(MH):
                ins = pool.tensor_scalar(alibi[:, h, :], distance, 2.0 ** (-8.0 * (h + 1) / MH), None, ALU.mult)
            ins.then_inc(alibi_ready, 1)
            pool.dma_start(fnorm[:], final_norm.partition_broadcast(P)).then_inc(fnorm_loaded, 16)
            pool.wait_ge(fnorm_loaded, 16)
            pool.tensor_scalar(fnorm[:], fnorm[:], float(D) ** 0.5, None, ALU.mult).then_inc(fnorm_scaled, 1)
            with pool.Fori(0, DEPTH) as l:
                norm(l * NORMS + 1)
                pool.wait_ge(o_ms, l + 1)
                pool.tensor_tensor(hrs[:], hms[:], neg_half[:], ALU.pow).then_inc(o_rstd, 1)
                norm(l * NORMS + 2)
                norm(l * NORMS + 3)

        @block.scalar
        def _(act):
            def split(s, n):
                act.wait_ge(raw_loaded[s], n * 16 + 16)
                act.wait_ge(unit_done[s], n + 1)
                act.activation(high[s][:], raw[s][:], ACT.Copy).then_inc(high_ready[s], 1)

            def square_sums(r, t):
                for n in range(2):
                    act.wait_ge(x_new, r * 4 + (2 * t + n + 1))
                    ins = act.activation(squares[2 * t + n], xs[:, t, 512 * n:512 * n + 512], ACT.Square,
                                         accum_out=ssq[:, t, n:n + 1])
                ins.then_inc(ssq_ready, 1)

            def norm_high(l, i, t, half):
                r = l * NORMS + i
                for b in (2 * half, 2 * half + 1):
                    act.wait_ge(x_turned, r * 8 + (4 * t + b + 1))
                    for e in range(2):
                        kt = 2 * b + e
                        ins = act.activation(act_h[:, kt, t * P:t * P + P], bank[T_BANKS[b]][:, e, t * P:t * P + P],
                                             ACT.Copy, scale=cur[:, C_NORM[i] + kt:C_NORM[i] + kt + 1])
                    ins.then_inc(act_high, 1)

            def norm(l, i, second):
                square_sums(l * NORMS + i, 0)
                act.wait_ge(cur_ready, l + 1)
                norm_high(l, i, 0, 0)
                norm_high(l, i, 0, 1)
                norm_high(l, i, 1, 0)
                split(*second)
                norm_high(l, i, 1, 1)
                square_sums(l * NORMS + i, 1)

            def ffn(f, l):
                q = (l * 2 + f) * FJ

                def silu(j):
                    act.wait_ge(gate_scaled, q + j + 1)
                    act.activation(silu_g, gate_in, ACT.Silu).then_inc(silu_ready, 1)

                def product_high(j, k0=0):
                    act.wait_ge(prod_ready, q + j + 1)
                    if k0 == 0:
                        s, n = ffn_unit(f, l, 2, j)
                        act.wait_ge(unit_done[s], n + 1)
                    act.activation(br_h[:, k0:k0 + 2, :], prod, ACT.Copy).then_inc(prod_high, 1)

                with act.Fori(0, FJ - 1) as j:
                    split(*ffn_unit(f, l, 0, j + 1))
                    silu(j)
                    split(*ffn_unit(f, l, 1, j + 1))
                    product_high(j)
                    split(*ffn_unit(f, l, 2, j))
                silu(FJ - 1)
                split(*ffn_unit(f, l, 2, FJ - 1))
                product_high(FJ - 1, 2)

            def mixer(l):
                def evict(u):
                    col, e = IN_UNITS[u]
                    s, n = mix_unit(l, u)
                    act.wait_ge(unit_done[s], n + 2)
                    if u == 0:
                        act.wait_ge(scale_ready, (l * NORMS + 2) * TT)
                    dst = {MV: val, HI: inp, HG: hg_sb[:]}[col][:, :, UC * e:UC * e + UC]
                    for t in range(TT):
                        ins = act.activation(dst[:, t, :], bank[u % 2][:, t, :], ACT.Copy, scale=scale_t[:, t:t + 1])
                    ins.then_inc(evicted_t, 1)

                def softmax_exp(h):
                    b = h % 2
                    act.wait_ge(s_max, l * MH + (h + 1))
                    act.activation(s_sb[:, b, 0:P], s_sb[:, b, 0:P], ACT.Exp, bias=nmax[:, b, 0:1],
                                   accum_out=psums[:, b, 0:1])
                    act.activation(s_sb[:, b, P:SW], s_sb[:, b, P:SW], ACT.Exp, bias=nmax[:, b, 1:2],
                                   accum_out=psums[:, b, 1:2]).then_inc(s_exp, 1)

                def probs_copy(h):
                    act.wait_ge(p_turned, l * MH + (h + 1))
                    if h >= 2:
                        act.wait_ge(pv_done, l * MH + (h - 1))
                    act.activation(pt_sb[:, h % 2, :], bank[4 + h % 2][:].rearrange("p a b -> p (a b)")[:, 0:SW],
                                   ACT.Copy).then_inc(pt_ready, 1)

                for u in range(U_B + 1):
                    if u == U_OUT + 6:
                        act.wait_ge(o_turned, l + 1)
                        for b in range(2):
                            act.activation(br_h[:, 2 * b:2 * b + 2, :], bank[2 + b][:], ACT.Copy,
                                           scale=cur[:, C_HN:C_HN + 1]).then_inc(o_high, 1)
                    split(*mix_unit(l, u + 2))
                    if u == U_OUT + 1:
                        act.wait_ge(o_done, l + 1)
                        for t in range(TT):
                            ins = act.activation(o_sb[:, t, :], bank[2 + t][:].rearrange("p a b -> p (a b)"),
                                                 ACT.Square)
                        ins.then_inc(o_squared, 1)
                    if U_SCORES + 2 <= u < U_SCORES + 2 + MH:
                        probs_copy(u - U_SCORES - 2)
                    if u < NIN and IN_UNITS[u][0] in TOKEN_MAJOR:
                        evict(u)
                    if u == taken(HF) - 1:
                        wait_evicted(act, l, u)
                        act.activation(t_sb[:], t_sb[:], ACT.Sigmoid).then_inc(f_squashed, 1)
                    if u == taken(HQ) - 1:
                        wait_evicted(act, l, u)
                        act.activation(q_sb[:], q_sb[:], ACT.Silu).then_inc(q_squashed, 1)
                    if U_SCORES <= u < U_SCORES + MH:
                        softmax_exp(u - U_SCORES)
                    if u == U_RAW:
                        wait_evicted(act, l, taken(HG) - 1)
                        act.activation(hg_sb[:], hg_sb[:], ACT.Silu).then_inc(hg_ready, 1)
                    if U_RAW < u < NIN:
                        first = U_GATE if u == U_RAW + 1 else u
                        g = gates[:, 2 * (first - U_GATE):2 * (u + 1 - U_GATE), :]
                        wait_evicted(act, l, u)
                        act.activation(g, g, ACT.Sigmoid).then_inc(gates_ready, 1)
                    if u == U_SCORES + MH + 3:
                        for b in range(2):
                            act.wait_ge(pv_done, l * MH + 4 * (b + 1))
                            act.activation(br_h[:, 4 + 2 * b:6 + 2 * b, :], bank[6 + b][:],
                                           ACT.Copy).then_inc(ob_high, 1)
                for u in range(U_B + 1, NMIX - 1):
                    split(*mix_unit(l, u + 2))
                    if u < U_WO + 1:
                        half = u - U_B - 1
                        act.wait_ge(merged, l * 2 + (half + 1))
                        act.activation(act_h[:, 4 * half:4 * half + 4, :], gates[:, 4 * half:4 * half + 4, :],
                                       ACT.Copy).then_inc(merged_high, 1)

            act.wait_ge(neg_half_set, 1)
            act.activation(table[:], neg_half[:, 0:1], ACT.Silu).then_inc(table_loaded, 1)

            def layer(l):
                ffn(0, l)
                split(*mix_unit(l, 0))
                norm(l, 1, mix_unit(l, 1))
                mixer(l)
                norm(l, 2, mix_unit(l, NMIX + 1))
                ffn(1, l)

            def split_half(s, half):
                v = slice(US // 2 * half, US // 2 * (half + 1))
                act.wait_ge((half_loaded[s], raw_loaded[s])[half], 16)
                act.activation(high[s][:, v], raw[s][:, v], ACT.Copy).then_inc((half_high[s], high_ready[s])[half], 1)

            act.wait_ge(first_cur_ready, 1)
            norm_high(0, 0, 0, 0)
            norm_high(0, 0, 0, 1)
            split_half(0, 0)
            norm_high(0, 0, 1, 0)
            split_half(0, 1)
            split_half(1, 0)
            norm_high(0, 0, 1, 1)
            split_half(1, 1)
            square_sums(0, 0)
            square_sums(0, 1)
            with act.Fori(0, DEPTH - 1) as l:
                layer(l)
                split(*ffn_unit(0, l + 1, 0, 0))
                norm(l + 1, 0, ffn_unit(0, l + 1, 1, 0))
            layer(DEPTH - 1)
            for t in range(TT):
                square_sums(DEPTH * NORMS, t)
                act.wait_ge(rstd_ready, DEPTH * NORMS * TT + t + 1)
                act.wait_ge(weights_done, 2 * t + 1)
                act.activation(xn[:, t, 0:512], xn[:, t, 0:512], ACT.Copy, scale=rstd[:, t:t + 1]).then_inc(y_ready[0], 1)

        @block.vector
        def _(dve):
            def split(s, n):
                dve.wait_ge(high_ready[s], n + 1)
                dve.tensor_tensor(low[s][:], raw[s][:], high[s][:].bitcast(F32),
                                  ALU.subtract).then_inc(low_ready[s], 1)

            def residual(l, i, t, n, factor=None):
                if t == 1 and n == 1:
                    s, last = mix_unit(l, NMIX - 1) if i == 1 else ffn_unit(i // 2, l, 2, FJ - 1)
                    dve.wait_ge(unit_done[s], last + 2)
                else:
                    dve.wait_ge(acc_done, l * 9 + (3 * i + 2 * t + n + 1))
                if factor is None:
                    factor = half_scale[:, t:t + 1]
                v = xs[:, t, 512 * n:512 * n + 512]
                dve.scalar_tensor_tensor(v, bank[2 + 2 * t + n][:].rearrange("p a b -> p (a b)"), factor, v,
                                         ALU.mult, ALU.add).then_inc(x_new, 1)

            def sum_up(r, t):
                dve.wait_ge(ssq_ready, r * TT + (t + 1))
                dve.tensor_scalar(msq[:, t:t + 1], ssq[:, t, 0:1], ssq[:, t, 1:2], D * EPS, ALU.add,
                                  ALU.add).then_inc(msq_ready, 1)

            def factors(r, t):
                dve.wait_ge(rstd_ready, r * TT + (t + 1))
                one = rstd[:, t:t + 1]
                dve.tensor_scalar(diag[:, t, :], ident[:], one, float(D) ** 0.5, ALU.mult, ALU.mult)
                dve.tensor_scalar(scale_t[:, t:t + 1], one, float(D) ** 0.5, None, ALU.mult)
                dve.tensor_scalar(half_scale[:, t:t + 1], one, 0.5 * float(D) ** 0.5, None,
                                  ALU.mult).then_inc(scale_ready, 1)

            def take_spread(r):
                dve.wait_ge(scale_spread, r + 1)
                dve.tensor_copy(scale_f[:], bank[T_BANKS[0]][:, 0, :]).then_inc(scale_f_ready, 1)

            def scaled(dst, src):
                return dve.tensor_tensor(dst, src, scale_f[:].rearrange("p (a t) -> p a t", a=1)
                                         .to_broadcast([P, dst.shape[1], S]), ALU.mult)

            def norm_low(l, i, t, half):
                r = l * NORMS + i
                for b in (2 * half, 2 * half + 1):
                    dve.wait_ge(act_high, r * 8 + (4 * t + b + 1))
                    for e in range(2):
                        kt = 2 * b + e
                        v = slice(t * P, t * P + P)
                        ins = dve.scalar_tensor_tensor(act_l[:, kt, v], bank[T_BANKS[b]][:, e, v],
                                                       cur[:, C_NORM[i] + kt:C_NORM[i] + kt + 1],
                                                       act_h[:, kt, v].bitcast(F32), ALU.mult, ALU.subtract)
                    ins.then_inc(act_low, 1)

            def norm(l, i, second, before, factor=None):
                r = l * NORMS + i
                residual(*before, 0, 0, factor)
                residual(*before, 0, 1, factor)
                residual(*before, 1, 0, factor)
                norm_low(l, i, 0, 0)
                norm_low(l, i, 0, 1)
                sum_up(r, 0)
                norm_low(l, i, 1, 0)
                residual(*before, 1, 1, factor)
                factors(r, 0)
                norm_low(l, i, 1, 1)
                split(*second)
                sum_up(r, 1)
                factors(r, 1)

            def ffn(f, l):
                q = (l * 2 + f) * FJ

                def product(j):
                    s, n = ffn_unit(f, l, 1, j)
                    dve.wait_ge(silu_ready, q + j + 1)
                    dve.wait_ge(unit_done[s], n + 2)
                    dve.wait_ge(prod_low, q + j + 1)
                    dve.tensor_tensor(prod, bank[1][:], silu_g, ALU.mult).then_inc(prod_ready, 1)

                def product_low(j, k0=0):
                    dve.wait_ge(prod_high, q + j + 1)
                    dve.tensor_tensor(br_l[:, k0:k0 + 2, :], prod, br_h[:, k0:k0 + 2, :].bitcast(F32),
                                      ALU.subtract).then_inc(prod_low, 1)

                def scale_gate(j):
                    s, n = ffn_unit(f, l, 0, j)
                    dve.wait_ge(unit_done[s], n + 2)
                    if isinstance(j, int) and j == 0:
                        scaled(gate_in[:, 0:1, :], bank[0][:, 0:1, :])
                        scaled(gate_in[:, 1:2, :], bank[4][:, 1:2, :]).then_inc(gate_scaled, 1)
                    else:
                        scaled(gate_in, bank[0][:]).then_inc(gate_scaled, 1)

                def step(j):
                    scale_gate(j)
                    product(j)
                    split(*ffn_unit(f, l, 1, j + 1))
                    product_low(j)
                    split(*ffn_unit(f, l, 2, j))

                split(*ffn_unit(f, l, 0, 1))
                take_spread(l * NORMS + 2 * f)
                dve.wait_ge(scale_f_ready, l * NORMS + 2 * f + 1)
                step(0)
                split(*ffn_unit(f, l, 0, 2))
                with dve.Fori(1, FJ - 2) as j:
                    step(j)
                    split(*ffn_unit(f, l, 0, j + 2))
                step(FJ - 2)
                scale_gate(FJ - 1)
                split(*ffn_unit(f, l, 2, FJ - 1))
                product(FJ - 1)
                product_low(FJ - 1, 2)

            def mixer(l):
                def level(i):
                    m = 1 if i == 0 else 1 << (i - 1)
                    dve.wait_ge(level_done, l * LEVELS + (i + 1))
                    dve.sem_inc(level_seen, 1)
                    if i == LEVELS - 1:
                        dve.tensor_copy(at[:, 2], bank[2][:].rearrange("p a (b t) -> p (a b) t", b=2)
                                        ).then_inc(level_taken, 1)
                        return
                    for t in range(TT):
                        if i == 0:
                            dst, mask = at[:, t], diag_mask.to_broadcast([P, HH, P])
                            src = bank[2 + t][:].rearrange("p a (b t) -> p (a b) t", b=2)
                        else:
                            dst = at[:, t].rearrange("p h (g e m) -> p h g e m", e=2, m=m)[:, :, :, 1, :]
                            mask = block_masks[:, i - 1:i, :].to_broadcast([P, HH, MC]).rearrange(
                                "p h (g m) -> p h g m", m=m)
                            src = bank[2 + t][:, 0, :].rearrange("p (h g m) -> p h g m", h=HH, m=m)
                        ins = dve.copy_predicated(dst, mask, src)
                    if i == 0:
                        dve.tensor_tensor(q_sb[:], q_sb[:], f_sb[:], ALU.mult).then_inc(level_taken, 1)
                        return
                    n = HH * S // m
                    tm = f_sb[:] if m == 1 else t_sb[:, HH * S - 2 * n:HH * S - n]
                    tb = tm.rearrange("p (g e) -> p g e", e=2)
                    qv = q_sb[:].rearrange("p (g e m) -> p g e m", e=2, m=m)
                    kv = k_sb[:].rearrange("p (g e m) -> p g e m", e=2, m=m)
                    if m > 1:
                        dve.wait_ge(level_t, l * (LEVELS - 3) + (i - 1))
                    if i < LEVELS - 2:
                        dve.tensor_tensor(t_sb[:, HH * S - n:HH * S - n // 2], tb[:, :, 0], tb[:, :, 1],
                                          ALU.mult).then_inc(level_t, 1)
                    dve.tensor_tensor(kv[:, :, 0, :], kv[:, :, 0, :], tb[:, :, 1:2].to_broadcast([P, n // 2, m]), ALU.mult)
                    dve.tensor_tensor(qv[:, :, 1, :], qv[:, :, 1, :], tb[:, :, 0:1].to_broadcast([P, n // 2, m]),
                                      ALU.mult).then_inc(level_taken, 1)

                def scores_max(h):
                    b = h % 2
                    dve.wait_ge(scores_done, l * MH + (h + 1))
                    if h >= 2:
                        dve.wait_ge(p_turned, l * MH + (h - 1))
                    dve.scalar_tensor_tensor(s_sb[:, b, :], bank[4 + b][:].rearrange("p a b -> p (a b)")[:, 0:SW],
                                             float(MD) ** -0.5, alibi[:, h, :], ALU.mult, ALU.add).then_inc(s_biased, 1)
                    dve.wait_ge(s_biased, l * MH + (h + 1))
                    dve.tensor_reduce(nmax[:, b, 0:1], s_sb[:, b, 0:P], AX, ALU.max, negate=True)
                    dve.tensor_reduce(nmax[:, b, 1:2], s_sb[:, b, P:SW], AX, ALU.max, negate=True).then_inc(s_max, 1)

                def probs_scale(h):
                    b = h % 2
                    dve.wait_ge(s_exp, l * MH + (h + 1))
                    dve.reciprocal(prec[:, b, :], psums[:, b, :]).then_inc(s_rec, 1)
                    dve.wait_ge(s_rec, l * MH + (h + 1))
                    dve.tensor_scalar(s_sb[:, b, 0:P], s_sb[:, b, 0:P], prec[:, b, 0:1], None, ALU.mult)
                    dve.tensor_scalar(s_sb[:, b, P:SW], s_sb[:, b, P:SW], prec[:, b, 1:2], None,
                                      ALU.mult).then_inc(p_ready, 1)

                def merged_split(half):
                    dve.wait_ge(merged_high, l * 2 + (half + 1))
                    dve.tensor_tensor(act_l[:, 4 * half:4 * half + 4, :], gates[:, 4 * half:4 * half + 4, :],
                                      act_h[:, 4 * half:4 * half + 4, :].bitcast(F32),
                                      ALU.subtract).then_inc(merged_low, 1)

                def evict(u):
                    col, e = IN_UNITS[u]
                    s, n = mix_unit(l, u)
                    dve.wait_ge(unit_done[s], n + 2)
                    if col in (HF, HQ):
                        buf = t_sb if col == HF else q_sb
                        dst = buf[:, 512 * e:512 * e + 512].rearrange("p (h t) -> p h t", h=2)
                    elif col in (MQ, MK):
                        dst = (mq_sb if col == MQ else mk_sb)[:, 2 * e:2 * e + 2, :]
                    else:
                        dst = gates[:, 2 * e:2 * e + 2, :]
                    scaled(dst, bank[u % 2][:]).then_inc(evicted_f, 1)

                for u in range(NMIX - 1):
                    if u == U_OUT + 6:
                        for b in range(2):
                            dve.wait_ge(o_high, l * 2 + (b + 1))
                            dve.scalar_tensor_tensor(br_l[:, 2 * b:2 * b + 2, :], bank[2 + b][:], cur[:, C_HN:C_HN + 1],
                                                     br_h[:, 2 * b:2 * b + 2, :].bitcast(F32), ALU.mult,
                                                     ALU.subtract).then_inc(o_low, 1)
                    if u == U_B + 1:
                        merged_split(0)
                    split(*mix_unit(l, u + 2))
                    if u == 0:
                        dve.wait_ge(bounds_ready, 1)
                        dve.tensor_copy(cur_lb[:], bounds[:, bass.ds(l, 1), :].rearrange("p l c -> p (l c)")
                                        ).then_inc(cur_lb_ready, 1)
                        take_spread(l * NORMS + 1)
                        dve.wait_ge(scale_f_ready, l * NORMS + 2)
                    if u < NIN and IN_UNITS[u][0] not in TOKEN_MAJOR:
                        evict(u)
                    if u == 3:
                        dve.wait_ge(cur_lb_ready, l + 1)
                        dve.wait_ge(f_squashed, l + 1)
                        for h in range(HH):
                            v = slice(h * S, h * S + S)
                            oml = cur_lb[:, C_OML + h:C_OML + h + 1]
                            ins = dve.tensor_scalar(f_sb[:, v], t_sb[:, v], oml, cur_lb[:, C_LB + h:C_LB + h + 1],
                                                    ALU.mult, ALU.add)
                            dve.tensor_scalar(k_sb[:, v], t_sb[:, v], 1.0, cur_lb[:, C_NOML + h:C_NOML + h + 1],
                                              ALU.subtract, ALU.mult)
                        ins.then_inc(forget_raw, 1)
                        dve.wait_ge(forget_raw, l + 1)
                        dve.tensor_scalar(f_sb[:], f_sb[:], MIN_FORGET, None, ALU.max).then_inc(decays_ready, 1)
                    if U_SCORES <= u < U_SCORES + MH:
                        scores_max(u - U_SCORES)
                    if U_LEVEL <= u < U_OUT:
                        if u == U_LEVEL:
                            dve.wait_ge(decays_ready, l + 1)
                        level(u - U_LEVEL)
                    if u == U_OUT + 2:
                        dve.wait_ge(o_squared, l + 1)
                        dve.tensor_reduce(hsq[:], t_sb[:].rearrange("p (g v) -> p g v", v=P), AX,
                                          ALU.add).then_inc(o_summed, 1)
                        dve.wait_ge(o_summed, l + 1)
                        dve.tensor_scalar(hms[:], hsq[:], 1.0 / P, EPS, ALU.mult, ALU.add).then_inc(o_ms, 1)
                    if u == U_OUT + 3:
                        dve.wait_ge(o_rstd, l + 1)
                        for t in range(TT):
                            ins = dve.tensor_tensor(o_sb[:, t, :].rearrange("p (h v) -> p h v", h=HH),
                                                    bank[2 + t][:].rearrange("p a (b v) -> p (a b) v", b=2),
                                                    hrs[:, HH * t:HH * t + HH].rearrange("p (h e) -> p h e", e=1)
                                                    .to_broadcast([P, HH, P]), ALU.mult)
                        ins.then_inc(o_scaled, 1)
                    if u == U_OUT + 4:
                        dve.wait_ge(o_scaled, l + 1)
                        dve.wait_ge(hg_ready, l + 1)
                        dve.tensor_tensor(o_sb[:], o_sb[:], hg_sb[:], ALU.mult).then_inc(o_gated, 1)
                    if U_SCORES <= u < U_SCORES + MH:
                        probs_scale(u - U_SCORES)
                    if u == U_SCORES + MH + 3:
                        for b in range(2):
                            dve.wait_ge(ob_high, l * 2 + (b + 1))
                            dve.tensor_tensor(br_l[:, 4 + 2 * b:6 + 2 * b, :], bank[6 + b][:],
                                              br_h[:, 4 + 2 * b:6 + 2 * b, :].bitcast(F32),
                                              ALU.subtract).then_inc(ob_low, 1)
                    if u in (U_A, U_A + 1):
                        half = u - U_A
                        s, n = mix_unit(l, u)
                        dve.wait_ge(unit_done[s], n + 2)
                        if half == 0:
                            dve.wait_ge(gates_ready, (l + 1) * (NIN - 1 - U_RAW))
                        for b in range(2):
                            g = gates[:, 4 * half + 2 * b:4 * half + 2 * b + 2, :]
                            dve.tensor_tensor(g, g, bank[2 - 2 * half + b][:], ALU.mult)
                    if u in (U_B, U_B + 1):
                        half = u - U_B
                        s, n = mix_unit(l, u)
                        dve.wait_ge(unit_done[s], n + 2)
                        for b in range(2):
                            g = gates[:, KT + 4 * half + 2 * b:KT + 4 * half + 2 * b + 2, :]
                            ins = dve.tensor_tensor(g, g, bank[4 + 2 * half + b][:], ALU.mult)
                        ins.then_inc(gated_b, 1)
                        dve.wait_ge(gated_b, l * 2 + (half + 1))
                        ga = gates[:, 4 * half:4 * half + 4, :]
                        dve.tensor_tensor(ga, ga, gates[:, KT + 4 * half:KT + 4 * half + 4, :],
                                          ALU.add).then_inc(merged, 1)
                    if u == U_WO:
                        merged_split(1)

            def take_norms(l):
                dve.tensor_copy(cur[:], par[:, bass.ds(l, 1), :].rearrange("p l c -> p (l c)")).then_inc(cur_ready, 1)

            def layer(l, nxt):
                ffn(0, l)
                split(*mix_unit(l, 0))
                norm(l, 1, mix_unit(l, 1), (l, 0))
                mixer(l)
                norm(l, 2, mix_unit(l, NMIX + 1), (l, 1), factor=1.0)
                if nxt:
                    take_norms(l + 1)
                ffn(1, l)

            def split_half(s, half):
                v = slice(US // 2 * half, US // 2 * (half + 1))
                dve.wait_ge((half_high[s], high_ready[s])[half], 1)
                dve.tensor_tensor(low[s][:, v], raw[s][:, v], high[s][:, v].bitcast(F32),
                                  ALU.subtract).then_inc((half_low, low_ready[s])[half], 1)

            dve.wait_ge(first_rows_turned, 1)
            dve.tensor_copy(cur[:, 0:KT], bank[5][:, 0, 0:KT]).then_inc(first_cur_ready, 1)
            dve.wait_ge(first_cur_ready, 1)
            norm_low(0, 0, 0, 0)
            norm_low(0, 0, 0, 1)
            split_half(0, 0)
            norm_low(0, 0, 1, 0)
            split_half(0, 1)
            dve.wait_ge(rows_turned, 1)
            pr = bank[5][:].rearrange("p a b -> p (a b)")
            for col, row, n in ((0, 0, KT), (KT, DEPTH * KT, KT), (2 * KT, 2 * DEPTH * KT, KT), (C_HN, 3 * DEPTH * KT, 1)):
                ins = dve.tensor_copy(par[:, :, col:col + n],
                                      pr[:, row:row + DEPTH * n].rearrange("p (l c) -> p l c", l=DEPTH))
            ins.then_inc(par_copied, 1)
            dve.tensor_copy(lbt[:, 0:DEPTH, :], pr[:, 3 * DEPTH * KT + DEPTH:DEPTH * PR].rearrange(
                "p (l c) -> p l c", l=DEPTH)).then_inc(lb_step, 1)
            dve.wait_ge(lb_step, 1)
            dve.tensor_tensor(lbt[:, 2, :], lbt[:, 0, :], lbt[:, 1, :], ALU.max).then_inc(lb_step, 1)
            dve.wait_ge(lb_step, 2)
            for i in range(DEPTH):
                ins = dve.tensor_tensor(lbt[:, i, :], lbt[:, i, :], lbt[:, 2, :], ALU.subtract)
            ins.then_inc(lb_diff, 1)
            dve.wait_ge(par_copied, 1)
            norm_low(0, 0, 1, 1)
            split_half(1, 0)
            split_half(1, 1)
            sum_up(0, 0)
            factors(0, 0)
            sum_up(0, 1)
            factors(0, 1)
            take_norms(0)
            with dve.Fori(0, DEPTH - 1) as l:
                layer(l, True)
                split(*ffn_unit(0, l + 1, 0, 0))
                norm(l + 1, 0, ffn_unit(0, l + 1, 1, 0), (l, 2))
            layer(DEPTH - 1, False)
            def weighted(t, n):
                residual(DEPTH - 1, 2, t, n)
                v = slice(512 * n, 512 * n + 512)
                dve.wait_ge(x_new, (DEPTH * NORMS * TT + t) * 2 + (n + 1))
                dve.tensor_tensor(xn[:, t, v], xs[:, t, v], fnorm[:, v], ALU.mult).then_inc(weights_done, 1)

            def scale_last(t):
                dve.wait_ge(rstd_ready, DEPTH * NORMS * TT + t + 1)
                dve.wait_ge(weights_done, 2 * t + 2)
                dve.tensor_scalar(xn[:, t, 512:], xn[:, t, 512:], rstd[:, t:t + 1], None,
                                  ALU.mult).then_inc(y_ready[1], 1)

            dve.wait_ge(fnorm_scaled, 1)
            weighted(0, 0)
            weighted(0, 1)
            sum_up(DEPTH * NORMS, 0)
            weighted(1, 0)
            scale_last(0)
            weighted(1, 1)
            sum_up(DEPTH * NORMS, 1)
            scale_last(1)

        @block.tensor
        def _(pe):
            def products(dst, left, right, first, last):
                pe.matmul(dst, left[0], right[0], start=first, stop=False)
                pe.matmul(dst, left[0], right[1], start=False, stop=False)
                return pe.matmul(dst, left[1], right[0], start=False, stop=last)

            def act_pair(k, cols):
                return act_h[:, k, cols], act_l[:, k, cols]

            def br_pair(k, cols):
                return br_h[:, k, cols], br_l[:, k, cols]

            def w_pair(s, start, n):
                return high[s][:, start:start + n], low[s][:, start:start + n]

            def cols(t):
                return slice(t * P, t * P + P)

            ALL = slice(0, S)

            def turns(r, t, half):
                pe.wait_ge(x_new, r * 4 + (2 * t + half + 1))
                for b in (2 * half, 2 * half + 1):
                    if t == 1:
                        pe.wait_ge(act_low, r * 8 + (b + 1))
                    for e in range(2):
                        kt = 2 * b + e
                        ins = pe.transpose(bank[T_BANKS[b]][:, e, cols(t)], xs[:, t, kt * P:kt * P + P], ident[:])
                    ins.then_inc(x_turned, 1)

            def spread(r):
                pe.wait_ge(ones_set, 1)
                for t in range(TT):
                    pe.wait_ge(scale_ready, r * TT + (t + 1))
                    ins = pe.matmul(bank[T_BANKS[0]][:, 0, cols(t)], ones[:], diag[:, t, :], start=True, stop=True)
                ins.then_inc(scale_spread, 1)

            def first_unit(s, n, r, token_major=False, start=False):
                if start:
                    pe.wait_ge(half_low, 1)
                else:
                    pe.wait_ge(low_ready[s], n + 2)
                order = ((0, 0), (0, 4), (1, 0), (1, 4)) if token_major else ((0, 0), (1, 0), (0, 4), (1, 4))
                for i, (g, k0) in enumerate(order):
                    if i == 1:
                        if start:
                            pe.wait_ge(rows_loaded, 80)
                            pe.transpose(bank[5][:].rearrange("p a b -> p (a b)")[:, 0:DEPTH * PR], rows[:],
                                         ident[0:DEPTH * PR, 0:DEPTH * PR]).then_inc(rows_turned, 1)
                        turns(r, 1, 1)
                    if start and i == 2:
                        pe.wait_ge(low_ready[s], n + 2)
                    for k in range(k0, k0 + 4):
                        if k % 2 == 0:
                            pe.wait_ge(act_low, r * 8 + (4 * (g if token_major else 1) + k // 2 + 1))
                        if token_major:
                            left, right = act_pair(k, cols(g)), w_pair(s, k * UC, UC)
                        else:
                            left, right = w_pair(s, k * UC + g * P, P), act_pair(k, ALL)
                        b = 4 if g == 1 and not token_major else 0
                        ins = products(bank[b][:, g, :], left, right, k == 0, k == KT - 1)
                ins.then_inc(unit_done[s], 1)

            def wide_unit(s, n, dst, token_major=False, spread_norm=None):
                pe.wait_ge(low_ready[s], n + 2)
                for g in range(2):
                    if g == 1 and spread_norm is not None:
                        spread(spread_norm)
                    for k in range(KT):
                        if token_major:
                            ins = products(dst[:, g, :], act_pair(k, cols(g)), w_pair(s, k * UC, UC), k == 0, k == KT - 1)
                        else:
                            ins = products(dst[:, g, :], w_pair(s, k * UC + g * P, P), act_pair(k, ALL), k == 0,
                                           k == KT - 1)
                ins.then_inc(unit_done[s], 1)

            def residual_quarter(s, pair, k0, t, h, first, last):
                for e in range(2):
                    ins = products(bank[2 + 2 * t + h][:].rearrange("p a b -> p (a b)"), pair(k0 + e, cols(t)),
                                   w_pair(s, e * D + h * 512, 512), first and e == 0, last and e == 1)
                return ins

            def residual_unit(s, n, pair, k0, first):
                pe.wait_ge(low_ready[s], n + 2)
                for t in range(TT):
                    for h in range(2):
                        ins = residual_quarter(s, pair, k0, t, h, first, False)
                ins.then_inc(unit_done[s], 1)

            def residual_tail(a, b, pair, ka, kb, r=None):
                for h in range(2):
                    residual_quarter(b[0], pair, kb, 0, h, False, True).then_inc(acc_done, 1)
                residual_quarter(a[0], pair, ka, 1, 0, False, False)
                residual_quarter(b[0], pair, kb, 1, 0, False, True).then_inc(acc_done, 1)
                if r is not None:
                    turns(r, 0, 0)
                    turns(r, 0, 1)
                residual_quarter(a[0], pair, ka, 1, 1, False, False).then_inc(unit_done[a[0]], 1)
                if r is not None:
                    turns(r, 1, 0)
                residual_quarter(b[0], pair, kb, 1, 1, False, True).then_inc(unit_done[b[0]], 1)

            def ffn(f, l, r):
                q = (l * 2 + f) * FJ

                def gate(j):
                    pe.wait_ge(gate_scaled, q + j)
                    wide_unit(*ffn_unit(f, l, 0, j), bank[0])

                def up(j):
                    pe.wait_ge(prod_ready, q + j)
                    wide_unit(*ffn_unit(f, l, 1, j), bank[1])

                def down(j, first=False):
                    pe.wait_ge(prod_low, q + j + 2)
                    residual_unit(*ffn_unit(f, l, 2, j), br_pair, 0, first)

                wide_unit(*ffn_unit(f, l, 1, 0), bank[1], spread_norm=l * NORMS + 2 * f)
                gate(1)
                up(1)
                down(0, first=True)
                with pe.Fori(2, FJ - 1) as j:
                    gate(j)
                    up(j)
                    down(j - 1)
                gate(FJ - 1)
                up(FJ - 1)
                pe.wait_ge(prod_low, q + FJ)
                a, b = ffn_unit(f, l, 2, FJ - 2), ffn_unit(f, l, 2, FJ - 1)
                pe.wait_ge(low_ready[a[0]], a[1] + 2)
                for h in range(2):
                    residual_quarter(a[0], br_pair, 0, 0, h, False, False)
                pe.wait_ge(prod_low, q + FJ + 1)
                pe.wait_ge(low_ready[b[0]], b[1] + 2)
                residual_tail(a, b, br_pair, 0, 2, r)

            def mixer(l):
                def level(i):
                    if i == 0:
                        pe.wait_ge(q_squashed, l + 1)
                        pe.wait_ge(decays_ready, l + 1)
                    else:
                        pe.wait_ge(level_taken, l * LEVELS + i)
                    if i == LEVELS - 1:
                        for h in range(HH):
                            ins = pe.matmul(bank[2][:, h // 2, cols(h % 2)], k_sb[:, h * S:h * S + P],
                                            q_sb[:, h * S + P:h * S + S], start=True, stop=True)
                    else:
                        for t in range(TT):
                            for h in range(HH):
                                v = slice(h * S + t * P, h * S + t * P + P)
                                if i == 0:
                                    dst, q = bank[2 + t][:, h // 2, cols(h % 2)], q_sb[:, v]
                                else:
                                    m = 1 << (i - 1)
                                    dst = bank[2 + t][:, 0, h * MC:h * MC + MC]
                                    q = q_sb[:, v].rearrange("p (g e m) -> p g e m", e=2, m=m)[:, :, 1, :]
                                ins = pe.matmul(dst, k_sb[:, v], q, start=True, stop=True)
                    ins.then_inc(level_done, 1)

                def hgrn_out():
                    pe.wait_ge(level_taken, l * LEVELS + LEVELS)
                    wait_evicted(pe, l, taken(HI) - 1)
                    for h in range(HH):
                        v = slice(h * P, h * P + P)
                        pe.matmul(bank[2][:, h // 2, cols(h % 2)], at[:, 0, h, :], inp[:, 0, v], start=True, stop=True)
                    for h in range(HH):
                        v = slice(h * P, h * P + P)
                        pe.matmul(bank[3][:, h // 2, cols(h % 2)], at[:, 2, h, :], inp[:, 0, v], start=True, stop=False)
                        ins = pe.matmul(bank[3][:, h // 2, cols(h % 2)], at[:, 1, h, :], inp[:, 1, v], start=False,
                                        stop=True)
                    ins.then_inc(o_done, 1)

                def hgrn_turns():
                    pe.wait_ge(o_gated, l + 1)
                    for h in range(HH):
                        for t in range(TT):
                            ins = pe.transpose(bank[2 + h // 2][:, h % 2, cols(t)], o_sb[:, t, h * P:h * P + P], ident[:])
                    ins.then_inc(o_turned, 1)

                def scores(h):
                    if h == 0:
                        wait_evicted(pe, l, taken(MK) - 1)
                    if h >= 2:
                        pe.wait_ge(pt_ready, l * MH + (h - 1))
                    v = slice(MD * (h % 2), MD * (h % 2) + MD)
                    b = bank[4 + h % 2][:].rearrange("p a b -> p (a b)")
                    pe.matmul(b[:, 0:P], mq_sb[v, h // 2, 0:P], mk_sb[v, h // 2, 0:P], start=True, stop=True)
                    pe.matmul(b[:, P:SW], mq_sb[v, h // 2, P:S], mk_sb[v, h // 2, :], start=True,
                              stop=True).then_inc(scores_done, 1)

                def probs_turns(h):
                    pe.wait_ge(p_ready, l * MH + (h + 1))
                    b = bank[4 + h % 2][:].rearrange("p a b -> p (a b)")
                    for c in range(3):
                        ins = pe.transpose(b[:, cols(c)], s_sb[:, h % 2, cols(c)], ident[:])
                    ins.then_inc(p_turned, 1)

                def values(h):
                    if h == 0:
                        wait_evicted(pe, l, taken(MV) - 1)
                    pe.wait_ge(pt_ready, l * MH + (h + 1))
                    dst = bank[6 + h // 4][MD * (h % 2):MD * (h % 2) + MD, (h // 2) % 2, :]
                    v = slice(MD * h, MD * h + MD)
                    pe.matmul(dst, val[:, 0, v], pt_sb[:, h % 2, 0:S], start=True, stop=False)
                    pe.matmul(dst[:, P:S], val[:, 1, v], pt_sb[:, h % 2, S:SW], start=False,
                              stop=True).then_inc(pv_done, 1)

                for u in range(NMIX - 1):
                    s, n = mix_unit(l, u)
                    if u == 0:
                        first_unit(s, n, l * NORMS + 1, token_major=True)
                    elif u < NIN:
                        if u >= 2:
                            wait_evicted(pe, l, u - 2)
                        wide_unit(s, n, bank[u % 2], token_major=IN_UNITS[u][0] in TOKEN_MAJOR,
                                  spread_norm=l * NORMS + 1 if u == 1 else None)
                    elif u < U_WO:
                        half = (u - U_A) % 2
                        if u == U_A:
                            pe.wait_ge(o_low, l * 2 + 2)
                        if u == U_A + 1:
                            wait_evicted(pe, l, NIN - 1)
                        if u == U_B:
                            pe.wait_ge(ob_low, l * 2 + 2)
                        pe.wait_ge(low_ready[s], n + 2)
                        b0, k0 = (2 - 2 * half, 0) if u < U_B else (4 + 2 * half, 4)
                        for m in range(4):
                            for k in range(4):
                                ins = products(bank[b0 + m // 2][:, m % 2, :], w_pair(s, k * 512 + m * P, P),
                                               br_pair(k0 + k, ALL), k == 0, k == 3)
                        ins.then_inc(unit_done[s], 1)
                    else:
                        i = u - U_WO
                        if i % 2 == 0:
                            pe.wait_ge(merged_low, l * 2 + (i // 2 + 1))
                        if i < 2:
                            residual_unit(s, n, act_pair, 2 * i, i == 0)
                        else:
                            b = mix_unit(l, u + 1)
                            pe.wait_ge(low_ready[s], n + 2)
                            for h in range(2):
                                residual_quarter(s, act_pair, 4, 0, h, False, False)
                            pe.wait_ge(low_ready[b[0]], b[1] + 2)
                            residual_tail((s, n), b, act_pair, 4, 6, l * NORMS + 2)
                    if U_SCORES + 2 <= u < U_SCORES + 2 + MH:
                        values(u - U_SCORES - 2)
                    if U_SCORES + 1 <= u < U_SCORES + 1 + MH:
                        probs_turns(u - U_SCORES - 1)
                    if U_SCORES <= u < U_SCORES + MH:
                        scores(u - U_SCORES)
                    if U_LEVEL <= u < U_OUT:
                        level(u - U_LEVEL)
                    if u == U_OUT:
                        hgrn_out()
                    if u == U_OUT + 5:
                        hgrn_turns()

            pe.wait_ge(ident_loaded, 16)
            pe.wait_ge(first_rows_loaded, 16)
            pe.transpose(bank[5][:, 0, 0:KT], first_rows[:], ident[0:KT, 0:KT]).then_inc(first_rows_turned, 1)
            turns(0, 0, 0)
            turns(0, 0, 1)
            turns(0, 1, 0)
            first_unit(*ffn_unit(0, 0, 0, 0), 0, start=True)

            def layer(l, r):
                ffn(0, l, l * NORMS + 1)
                mixer(l)
                first_unit(*ffn_unit(1, l, 0, 0), l * NORMS + 2)
                ffn(1, l, r)

            with pe.Fori(0, DEPTH - 1) as l:
                layer(l, (l + 1) * NORMS)
                first_unit(*ffn_unit(0, l + 1, 0, 0), (l + 1) * NORMS)
            layer(DEPTH - 1, None)


_INS = ['x', 'ffn1_norm', 'ffn1_w_gu', 'ffn1_w_down', 'mix_norm', 'w_in', 'hgrn_lb_logits', 'hgrn_norm', 'w_branch_a',
        'w_branch_b', 'w_out', 'ffn2_norm', 'ffn2_w_gu', 'ffn2_w_down', 'final_norm']


def kernel(**inputs):
    import numpy as _np
    import concourse.bacc as _bacc
    from concourse.bass_utils import run_bass_kernel_spmd as _run

    nc = _bacc.Bacc("TRN2", target_bir_lowering=False, num_devices=1)
    arrays, args = {}, []
    for name in _INS:
        a = _np.ascontiguousarray(inputs[name])
        arrays[f"in_{name}"] = a
        args.append(nc.dram_tensor(f"in_{name}", a.shape, mybir.dt.from_np(a.dtype), kind="ExternalInput").ap())
    key, query = _np.arange(P)[None, :], _np.arange(P)[:, None]
    same = key - query
    causal = _np.where(same <= 0, same, -4e11)
    src, dst = query, key
    masks = [src == dst]
    for i in range(NMASK - 1):
        m = 1 << i
        mask = (src // (2 * m) == dst // (2 * m)) & (src // m % 2 == 0)
        masks.append(mask[:, _np.arange(P) // m % 2 == 1])
    consts = _np.concatenate([_np.eye(P), causal, same - P, causal] + masks, axis=1).astype(_np.float32)
    arrays["shape_consts"] = consts
    args.append(nc.dram_tensor("shape_consts", consts.shape, F32, kind="ExternalInput").ap())
    args.append(nc.dram_tensor("out_0", (1, S, D), F32, kind="ExternalOutput").ap())
    build(nc, *args)
    r = _run(nc, [arrays], core_ids=[0])
    return r.results[0]["out_0"]
```
